# Optimizing a Trainium2 kernel written in Bass

```python
import jax, jax.numpy as jnp
from jax import lax
import numpy as np

D_MODEL = 1024
BATCH = 1
SEQ = 256
DEPTH = 1

N_HEADS = 8
HEAD_DIM = 64
ATTN_WIDTH = N_HEADS * HEAD_DIM
CONV_WIDTH = D_MODEL // 2
CONV_KERNEL = 31
MOBA_BLOCK = 256
MOBA_TOPK = 3
Q_CHUNK = 64
D_FF = 4 * D_MODEL
EPS = 1e-6
IN_COLS = 3 * ATTN_WIDTH + 2 * CONV_WIDTH + 2 * D_MODEL

kernel_name = "hybrid_moba_conformer_conv_block"

def rmsnorm(x, g):
    xf = x.astype(jnp.float32)
    y = xf * lax.rsqrt(jnp.mean(xf * xf, axis=-1, keepdims=True) + EPS)
    return (y * g.astype(jnp.float32)).astype(x.dtype)

def layernorm(x, g, b):
    xf = x.astype(jnp.float32)
    mu = jnp.mean(xf, axis=-1, keepdims=True)
    var = jnp.mean(jnp.square(xf - mu), axis=-1, keepdims=True)
    y = (xf - mu) * lax.rsqrt(var + EPS)
    return (y * g.astype(jnp.float32) + b.astype(jnp.float32)).astype(x.dtype)

def gather_blocks(blocks, idx):
    return jax.vmap(jax.vmap(lambda bl, ix: bl[ix]))(blocks, idx)

def moba_attention(q, k, v):
    b, h, s, dh = q.shape
    nb = -(-s // MOBA_BLOCK)
    s_pad = nb * MOBA_BLOCK
    pad = [(0, 0), (0, 0), (0, s_pad - s), (0, 0)]
    kb = jnp.pad(k, pad).reshape(b, h, nb, MOBA_BLOCK, dh)
    vb = jnp.pad(v, pad).reshape(b, h, nb, MOBA_BLOCK, dh)
    scale = dh ** -0.5
    k_mean = jnp.mean(kb.astype(jnp.float32), axis=3)
    gate = jnp.einsum('bhsd,bhnd->bhsn', q.astype(jnp.float32), k_mean)
    q_blk = jnp.arange(s) // MOBA_BLOCK
    past = jnp.arange(nb)[None, :] < q_blk[:, None]
    gate = jnp.where(past, gate, -jnp.inf)
    k_sel = max(1, min(MOBA_TOPK, nb - 1))
    top_val, top_idx = lax.top_k(gate, k_sel)
    sel_valid = jnp.isfinite(top_val)
    pos_in_block = jnp.arange(MOBA_BLOCK)
    n_chunks = s // Q_CHUNK

    def chunk(i):
        s0 = i * Q_CHUNK
        qc = lax.dynamic_slice_in_dim(q, s0, Q_CHUNK, axis=2)
        idx = lax.dynamic_slice_in_dim(top_idx, s0, Q_CHUNK, axis=2)
        ok = lax.dynamic_slice_in_dim(sel_valid, s0, Q_CHUNK, axis=2)
        k_g = gather_blocks(kb, idx)
        v_g = gather_blocks(vb, idx)
        own = s0 // MOBA_BLOCK
        k_own = lax.dynamic_index_in_dim(kb, own, axis=2, keepdims=False)
        v_own = lax.dynamic_index_in_dim(vb, own, axis=2, keepdims=False)
        l_sel = jnp.einsum('bhcd,bhckld->bhckl', qc, k_g).astype(jnp.float32) * scale
        l_sel = jnp.where(ok[..., None], l_sel, -jnp.inf)
        l_own = jnp.einsum('bhcd,bhld->bhcl', qc, k_own).astype(jnp.float32) * scale
        qpos = s0 + jnp.arange(Q_CHUNK)
        causal = (own * MOBA_BLOCK + pos_in_block)[None, :] <= qpos[:, None]
        l_own = jnp.where(causal, l_own, -jnp.inf)
        logits = jnp.concatenate([l_sel.reshape(b, h, Q_CHUNK, k_sel * MOBA_BLOCK), l_own], axis=-1)
        p = jax.nn.softmax(logits, axis=-1)
        p_sel = p[..., :k_sel * MOBA_BLOCK].reshape(b, h, Q_CHUNK, k_sel, MOBA_BLOCK)
        p_own = p[..., k_sel * MOBA_BLOCK:]
        o = (jnp.einsum('bhckl,bhckld->bhcd', p_sel, v_g.astype(jnp.float32))
             + jnp.einsum('bhcl,bhld->bhcd', p_own, v_own.astype(jnp.float32)))
        return o.astype(q.dtype)

    out = lax.map(chunk, jnp.arange(n_chunks))
    return out.transpose(1, 2, 0, 3, 4).reshape(b, h, s, dh)

def conformer_conv(u, w_dw, b_dw, ln_g, ln_b):
    a, g = jnp.split(u, 2, axis=-1)
    z = a * jax.nn.sigmoid(g)
    z = lax.conv_general_dilated(
        z, w_dw[:, None, :].astype(z.dtype), window_strides=(1,),
        padding=[(CONV_KERNEL - 1, 0)],
        dimension_numbers=('NWC', 'WIO', 'NWC'),
        feature_group_count=CONV_WIDTH) + b_dw
    z = layernorm(z, ln_g, ln_b)
    return jax.nn.silu(z)

def setup_inputs(seed: int = 0) -> dict:
    key = jax.random.key(seed)
    ks = jax.random.split(key, 20)
    n = jax.random.normal
    f = jnp.float32
    return {
        "x": n(ks[0], (BATCH, SEQ, D_MODEL), f),
        "g_mix": 1.0 + 0.02 * n(ks[1], (DEPTH, D_MODEL), f),
        "w_in": n(ks[2], (DEPTH, D_MODEL, IN_COLS), f) * D_MODEL ** -0.5,
        "b_glu": 0.02 * n(ks[3], (DEPTH, 2 * CONV_WIDTH), f),
        "w_dw": n(ks[4], (DEPTH, CONV_KERNEL, CONV_WIDTH), f) * CONV_KERNEL ** -0.5,
        "b_dw": 0.02 * n(ks[5], (DEPTH, CONV_WIDTH), f),
        "ln_g": 1.0 + 0.02 * n(ks[6], (DEPTH, CONV_WIDTH), f),
        "ln_b": 0.02 * n(ks[7], (DEPTH, CONV_WIDTH), f),
        "w_conv_pw": n(ks[8], (DEPTH, CONV_WIDTH, D_MODEL), f) * CONV_WIDTH ** -0.5,
        "b_conv_pw": 0.02 * n(ks[9], (DEPTH, D_MODEL), f),
        "w_attn_up": n(ks[10], (DEPTH, ATTN_WIDTH, D_MODEL), f) * ATTN_WIDTH ** -0.5,
        "w_out": n(ks[11], (DEPTH, D_MODEL, D_MODEL), f) * D_MODEL ** -0.5,
        "g_ffn": 1.0 + 0.02 * n(ks[12], (DEPTH, D_MODEL), f),
        "w_ff1": n(ks[13], (DEPTH, D_MODEL, D_FF), f) * D_MODEL ** -0.5,
        "w_ff2": n(ks[14], (DEPTH, D_FF, D_MODEL), f) * D_FF ** -0.5,
        "g_final": 1.0 + 0.02 * n(ks[15], (D_MODEL,), f),
    }

def reference(x, g_mix, w_in, b_glu, w_dw, b_dw, ln_g, ln_b, w_conv_pw, b_conv_pw,
              w_attn_up, w_out, g_ffn, w_ff1, w_ff2, g_final):
    b, s, _ = x.shape
    c_q = ATTN_WIDTH
    c_k = 2 * ATTN_WIDTH
    c_v = 3 * ATTN_WIDTH
    c_u = c_v + 2 * CONV_WIDTH
    c_ga = c_u + D_MODEL
    for l in range(DEPTH):
        h = rmsnorm(x, g_mix[l])
        proj = h @ w_in[l]
        q = proj[..., :c_q].reshape(b, s, N_HEADS, HEAD_DIM).transpose(0, 2, 1, 3)
        k = proj[..., c_q:c_k].reshape(b, s, N_HEADS, HEAD_DIM).transpose(0, 2, 1, 3)
        v = proj[..., c_k:c_v].reshape(b, s, N_HEADS, HEAD_DIM).transpose(0, 2, 1, 3)
        u = proj[..., c_v:c_u] + b_glu[l]
        gate_a = jax.nn.sigmoid(proj[..., c_u:c_ga])
        gate_c = jax.nn.sigmoid(proj[..., c_ga:])
        o = moba_attention(q, k, v).transpose(0, 2, 1, 3).reshape(b, s, ATTN_WIDTH)
        branch_a = o @ w_attn_up[l]
        cz = conformer_conv(u, w_dw[l], b_dw[l], ln_g[l], ln_b[l])
        branch_c = cz @ w_conv_pw[l] + b_conv_pw[l]
        merged = gate_a * branch_a + gate_c * branch_c
        x = x + merged @ w_out[l]
        h = rmsnorm(x, g_ffn[l])
        x = x + jnp.square(jax.nn.relu(h @ w_ff1[l])) @ w_ff2[l]
    return rmsnorm(x, g_final)


_drawn_inputs = setup_inputs


def setup_inputs(seed=0):
    import zlib

    import numpy as np

    out = dict(_drawn_inputs(seed))
    spreads = {}
    factors = {'g_mix': 6.01,
     'b_glu': 8.0,
     'b_dw': 12.966,
     'ln_g': 26.14,
     'ln_b': 26.5,
     'b_conv_pw': 18.977,
     'g_ffn': 8.832,
     'g_final': 8.102}
    for name, (base, spread) in spreads.items():
        noise = np.random.default_rng([zlib.crc32(name.encode()), seed]).standard_normal(out[name].shape)
        drawn = base * np.exp(spread * noise) if base else spread * noise
        out[name] = __import__('jax').numpy.asarray(drawn.astype(out[name].dtype))
    for name, factor in factors.items():
        out[name] = (out[name] * factor).astype(out[name].dtype)
    return out
```

```python
from contextlib import ExitStack

import concourse.bass as bass
from concourse import mybir

P = 128
T = 256
TT = T // P
D = 1024
KD = D // P
HEADS, HD = 8, 64
A = HEADS * HD
C = D // 2
CC = C // P
TAPS = 31
F = 4 * D
W = 512
HK = 4
EPS = 1e-6
SCALE = HD ** -0.5
MASKED = -1e30

SLOTS = 4
AHEAD = 2

ORDER = [3, 4, 0, 1, 2, 5, 6, 7, 8]
UG, Q, K, V, GA, GC = 1, 2, 3, 4, 5, 7
U_ATTN = 2 * len(ORDER)
U_CONV = U_ATTN + 2
U_OUT = U_CONV + 2
U_FF = U_OUT + 4
FB = F // W
U_LOOP = U_FF + 2
U_LAST = U_LOOP + 4 * (FB - 1)
UNITS = U_LAST + 2
assert U_LOOP % SLOTS == 0

S_GLU = 4
S_QT, S_KT = 6, 8
S_ATT = 9
PAIRS = HEADS // 2
S_OT = S_ATT + 6
S_LN = 17
TAPS_AT = {5: 32, 6: 32, 7: 32, 8: 32, 9: 16, 10: 16, 11: 16, 12: 16, 13: 20, 14: 28, 15: 30, 16: 32}
POOL_LO = (7, 10, 13, 16, 19)

F32 = mybir.dt.float32
F32R = mybir.dt.float32r
BF16 = mybir.dt.bfloat16
ALU = mybir.AluOpType
ACT = mybir.ActivationFunctionType
AX = mybir.AxisListType

V_GMIX, V_BGLU, V_BDW, V_LNG, V_LNB, V_GFFN = 0, 8, 16, 20, 24, 28
VROWS = 36


def conv_share(step):
    total = TAPS * CC
    first = 0
    for s in sorted(TAPS_AT):
        if s == step:
            return first, first + TAPS_AT[s] * total // sum(TAPS_AT.values())
        first += TAPS_AT[s] * total // sum(TAPS_AT.values())
    return (first, total) if step == S_LN else (0, 0)


def low_count(n):
    pool = sum(1 for u in POOL_LO if u <= n)
    return n + 1 - pool, pool


def build(nc, x, g_mix, w_in, b_glu, w_dw, b_dw, ln_g, ln_b, w_conv_pw, b_conv_pw,
          w_attn_up, w_out, g_ffn, w_ff1, w_ff2, g_final, out):
    x_v = x.rearrange("b (t p) d -> p (b t) d", p=P)
    out_v = out.rearrange("b (t p) d -> p (b t) d", p=P)
    win_v = w_in.rearrange("l (c p) n -> p (l c) n", p=P)
    wattn_v = w_attn_up.rearrange("l (c p) n -> p (l c) n", p=P)
    wconv_v = w_conv_pw.rearrange("l (c p) n -> p (l c) n", p=P)
    wout_v = w_out.rearrange("l (c p) n -> p (l c) n", p=P)
    wff1_v = w_ff1.rearrange("l (c p) n -> p (l c) n", p=P)
    wff2_v = w_ff2.rearrange("l (f c p) n -> (l f) p c n", p=P, c=HK)

    def unit_source(n):
        if n < U_ATTN:
            b, half = divmod(n, 2)
            return win_v[:, HK * half:HK * half + HK, ORDER[b] * W:ORDER[b] * W + W]
        if n < U_OUT:
            v = wattn_v if n < U_CONV else wconv_v
            col = (n - U_ATTN) % 2
            return v[:, :, col * W:col * W + W]
        if n < U_FF:
            half, col = divmod(n - U_OUT, 2)
            return wout_v[:, HK * half:HK * half + HK, col * W:col * W + W]
        return wff1_v[:, HK * (n - U_FF):HK * (n - U_FF) + HK, 0:W]

    with ExitStack() as ctx:
        def sb(name, shape, dt=F32):
            return ctx.enter_context(nc.sbuf_tensor(name, shape, dt))

        def sem(name):
            return ctx.enter_context(nc.semaphore(name))

        raw = sb("raw", [P, SLOTS, HK, W])
        w_hi = sb("w_hi", [P, SLOTS, HK, W], F32R)
        w_lo = sb("w_lo", [P, SLOTS, HK, W], F32R)
        a_hi = sb("a_hi", [P, KD, T], F32R)
        a_lo = sb("a_lo", [P, KD, T], F32R)
        b_hi = sb("b_hi", [P, KD, T], F32R)
        b_lo = sb("b_lo", [P, KD, T], F32R)
        res = sb("res", [P, TT, D])
        nat = sb("nat", [P, TT, D])
        gates = sb("gates", [P, 2, TT, D])
        v_nat = sb("v_nat", [P, TT, A])
        qk_t = sb("qk_t", [P, 2, CC, T])
        probs = sb("probs", [P, 768])
        probs_t = sb("probs_t", [P, 768])
        o_nat = sb("o_nat", [P, TT, A])
        PAD = TAPS - 1
        z = sb("z", [P, CC, PAD + T])
        conv = sb("conv", [P, CC, T])
        zn = sb("zn", [P, TT, C])
        vec_rows = sb("vec_rows", [VROWS, P])
        dw_rows = sb("dw_rows", [TAPS * CC, P])
        vec = sb("vec", [P, VROWS])
        dw = sb("dw", [P, TAPS * CC])
        gfin_bc = sb("gfin_bc", [P, D])
        bpw_bc = sb("bpw_bc", [P, D])
        ident = sb("ident", [P, P])
        ident_b = sb("ident_b", [P, P], BF16)
        mask_b = sb("mask_b", [P, T], BF16)
        zero_b = sb("zero_b", [P, W], BF16)
        sq_sum = sb("sq_sum", [P, 3, 4])
        ms = sb("ms", [P, 3, TT])
        root = sb("root", [P, 4, TT])
        rstd = sb("rstd", [P, 4, TT])
        stats = sb("stats", [P, TT, 6])
        mean_var = sb("mean_var", [P, TT, 2])
        ln_var = sb("ln_var", [P, TT])
        smax = sb("smax", [P, PAIRS, 4])
        nbias = sb("nbias", [P, PAIRS, 4])
        psums = sb("psums", [P, PAIRS, 4])
        rinv = sb("rinv", [P, PAIRS, 4])
        silu_x = zn[:, :, :].rearrange("p t c -> p (t c)").rearrange("p (c t) -> p c t", c=CC)
        gcb = qk_t[:, :, :, :].rearrange("p a c t -> p (a c t)").rearrange("p (t d) -> p t d", t=TT)

        ps = ctx.enter_context(nc.psum_tensor("ps", [P, 8, W], F32))
        TB, SB0 = 4, 6

        def chunks(bank):
            return ps[:, bank:bank + 2, :].rearrange("p b n -> p (b n)").rearrange("p (c t) -> p c t", c=4)

        raw_full = [sem(f"raw_full{i}") for i in range(SLOTS)]
        x_full = sem("x_full")
        vec_full = sem("vec_full")
        bc_full = sem("bc_full")
        hi_made = sem("hi_made")
        lo_made = sem("lo_made")
        lo_made_pool = sem("lo_made_pool")
        used = sem("used")
        const_made = sem("const_made")
        ident_made = sem("ident_made")
        vec_tr = sem("vec_tr")
        vec_made = sem("vec_made")
        x_tr = sem("x_tr")
        xt_hi = sem("xt_hi")
        xt_lo = sem("xt_lo")
        sq_made = sem("sq_made")
        ms_made = sem("ms_made")
        root_made = sem("root_made")
        rstd_made = sem("rstd_made")
        evac = sem("evac")
        glu_tr = sem("glu_tr")
        glu_sig = sem("glu_sig")
        z_made = sem("z_made")
        conv_step = sem("conv_step")
        conv_tr = sem("conv_tr")
        ln_chain = sem("ln_chain")
        zn_made = sem("zn_made")
        zn_tr = sem("zn_tr")
        silu_sig = sem("silu_sig")
        silu_made = sem("silu_made")
        cz_hi = sem("cz_hi")
        cz_lo = sem("cz_lo")
        qk_tr = sem("qk_tr")
        qk_made = sem("qk_made")
        scored = sem("scored")
        max_made = sem("max_made")
        bias_made = sem("bias_made")
        exp_made = sem("exp_made")
        p_tr = sem("p_tr")
        pt_made = sem("pt_made")
        pv_done = sem("pv_done")
        rinv_made = sem("rinv_made")
        o_made = sem("o_made")
        o_tr = sem("o_tr")
        o_hi = sem("o_hi")
        o_lo = sem("o_lo")
        gcb_made = sem("gcb_made")
        m_attn = sem("m_attn")
        m_bias = sem("m_bias")
        m_conv = sem("m_conv")
        merged = sem("merged")
        m_tr = sem("m_tr")
        m_hi = sem("m_hi")
        m_lo = sem("m_lo")
        res2 = sem("res2")
        h_tr = sem("h_tr")
        h_hi = sem("h_hi")
        h_lo = sem("h_lo")
        relu_made = sem("relu_made")
        sq_hidden = sem("sq_hidden")
        f_tr = sem("f_tr")
        f_hi = sem("f_hi")
        f_lo = sem("f_lo")
        ff_done = sem("ff_done")
        y_made = sem("y_made")
        out_made = sem("out_made")
        stored = sem("stored")

        block = ctx.enter_context(nc.Block())

        @block.sync
        def _(sp):
            def load(n, source):
                if n >= SLOTS:
                    dve, pool = low_count(n - SLOTS)
                    sp.wait_ge(lo_made, dve)
                    if pool:
                        sp.wait_ge(lo_made_pool, pool)
                sp.dma_start(raw[:, n % SLOTS], source).then_inc(raw_full[n % SLOTS], 16)

            for n in range(U_LOOP):
                load(n, unit_source(n))
            pools = len(POOL_LO)
            with sp.Fori(0, FB - 1) as i:
                for j in range(4):
                    if j < 2:
                        source = wff1_v[:, HK * j:HK * j + HK, bass.ds(i * W + W, W)]
                    else:
                        source = wff2_v[bass.ds(i, 1), :, :, (j - 2) * W:(j - 1) * W].rearrange("f p c n -> p (f c) n")
                    sp.wait_ge(lo_made, i * 4 + (U_LOOP + j - SLOTS + 1 - pools))
                    sp.dma_start(raw[:, j], source).then_inc(raw_full[j], 16)
            for j in range(2):
                load(U_LAST + j, wff2_v[FB - 1, :, :, j * W:j * W + W])
            for t in range(TT):
                sp.wait_ge(out_made, t + 1)
                sp.dma_start(out_v[:, t], res[:, t]).then_inc(stored, 16)
            sp.wait_ge(stored, 16 * TT)

        @block.gpsimd
        def _(pool):
            nc.gpsimd.memset(ident[:], 0.0).then_inc(const_made, 1)
            nc.gpsimd.memset(mask_b[:], 0.0).then_inc(const_made, 1)
            nc.gpsimd.memset(zero_b[:], 0.0).then_inc(const_made, 1)
            nc.gpsimd.memset(z[:, :, 0:PAD], 0.0).then_inc(const_made, 1)
            pool.wait_ge(const_made, 1)
            nc.gpsimd.affine_select(out=ident[:], in_=ident[:], compare_op=ALU.not_equal, fill=1.0, base=0,
                                    pattern=[[-1, P]], channel_multiplier=1).then_inc(ident_made, 1)
            pool.wait_ge(const_made, 2)
            nc.gpsimd.affine_select(out=mask_b[:], in_=mask_b[:], compare_op=ALU.is_ge, fill=MASKED, base=P,
                                    pattern=[[-1, T]], channel_multiplier=1).then_inc(ident_made, 1)
            pool.wait_ge(ident_made, 1)
            nc.gpsimd.tensor_copy(ident_b[:], ident[:]).then_inc(ident_made, 1)

            def low(n):
                pool.wait_ge(hi_made, n + 1)
                nc.gpsimd.tensor_tensor(w_lo[:, n % SLOTS], raw[:, n % SLOTS], w_hi[:, n % SLOTS].bitcast(F32),
                                        ALU.subtract).then_inc(lo_made_pool, 1)

            for n in POOL_LO:
                if n < U_ATTN:
                    low(n)
            pool.wait_ge(bc_full, 32)
            pool.wait_ge(scored, PAIRS)
            pool.wait_ge(evac, len(ORDER))
            for t in range(TT):
                nc.gpsimd.tensor_tensor(gcb[:, t], gates[:, 1, t], bpw_bc[:], ALU.mult).then_inc(gcb_made, 1)
            for n in POOL_LO:
                if n >= U_ATTN:
                    low(n)
            for col in range(2):
                pool.wait_ge(m_attn, col + 1)
                pool.wait_ge(gcb_made, TT)
                part = nat[:, :, col * W:col * W + W]
                nc.gpsimd.tensor_tensor(part, part, gcb[:, :, col * W:col * W + W], ALU.add).then_inc(m_bias, 1)
            pool.wait_ge(relu_made, 1)
            nc.gpsimd.tensor_tensor(nat[:, :, W:D], nat[:, :, 0:W], nat[:, :, 0:W], ALU.mult).then_inc(sq_hidden, 1)
            with pool.Fori(1, FB) as i:
                pool.wait_ge(relu_made, i + 1)
                pool.wait_ge(f_tr, i)
                nc.gpsimd.tensor_tensor(nat[:, :, W:D], nat[:, :, 0:W], nat[:, :, 0:W], ALU.mult).then_inc(sq_hidden, 1)

        @block.scalar
        def _(act):
            for t in range(TT):
                act.dma_start(res[:, t], x_v[:, t]).then_inc(x_full, 16)
            for row, v in ((V_GMIX, g_mix), (V_BGLU, b_glu), (V_BDW, b_dw), (V_LNG, ln_g), (V_LNB, ln_b), (V_GFFN, g_ffn)):
                rows = v.shape[1] // P
                act.dma_start(vec_rows[row:row + rows, :], v.rearrange("l (c p) -> (l c) p", p=P)).then_inc(vec_full, 16)
            act.dma_start(dw_rows[:], w_dw.rearrange("l j (c p) -> (l j c) p", p=P)).then_inc(vec_full, 16)
            act.dma_start(bpw_bc[:], b_conv_pw.to_broadcast([P, D])).then_inc(bc_full, 16)
            act.dma_start(gfin_bc[:], g_final.rearrange("(a d) -> a d", a=1).to_broadcast([P, D])).then_inc(bc_full, 16)

            def high(n):
                act.wait_ge(raw_full[n % SLOTS], 16 * (n // SLOTS + 1))
                if n >= SLOTS:
                    act.wait_ge(used, n - SLOTS + 1)
                nc.scalar.copy(w_hi[:, n % SLOTS], raw[:, n % SLOTS]).then_inc(hi_made, 1)

            act.wait_ge(vec_tr, 1)
            nc.scalar.copy(vec[:], ps[:, TB, 0:VROWS]).then_inc(vec_made, 1)
            nc.scalar.copy(dw[:], ps[:, TB, P:P + TAPS * CC]).then_inc(vec_made, 1)
            act.wait_ge(vec_made, 1)
            for half in range(2):
                act.wait_ge(x_tr, half + 1)
                for c in range(4):
                    k = 4 * half + c
                    nc.scalar.activation(a_hi[:, k], chunks(TB if half == 0 else 2)[:, c], ACT.Copy,
                                         scale=vec[:, V_GMIX + k:V_GMIX + k + 1]).then_inc(xt_hi, 1)
                if half == 0:
                    high(0)
            for t in range(TT):
                act.wait_ge(x_full, 16 * TT)
                nc.scalar.activation(nat[:, t], res[:, t], ACT.Square, accum_out=sq_sum[:, 0, t:t + 1]).then_inc(sq_made, 1)
            high(1)
            act.wait_ge(ms_made, 1)
            nc.scalar.activation(root[:, 0], ms[:, 0], ACT.Sqrt).then_inc(root_made, 1)

            def take(b):
                bank = 2 * (b % 2)
                act.wait_ge(used, 2 * b + 2)
                if b == 0:
                    act.wait_ge(rstd_made, 1)
                if b == Q:
                    act.wait_ge(glu_tr, CC)
                if b < 2 or b in (Q, K):
                    dst, fn = nat[:, :, (b % 2) * W:(b % 2) * W + W], ACT.Copy
                elif b == V:
                    dst, fn = v_nat[:], ACT.Copy
                else:
                    g, col = divmod(b - GA, 2)
                    dst, fn = gates[:, g, :, col * W:col * W + W], ACT.Sigmoid
                for t in range(TT):
                    last = nc.scalar.activation(dst[:, t], ps[:, bank + t], fn, scale=rstd[:, 0, t:t + 1])
                last.then_inc(evac, 1)

            def qk_out(i, bank):
                act.wait_ge(qk_tr, i + 1)
                nc.scalar.copy(qk_t[:, i], chunks(bank)).then_inc(qk_made, 1)

            def exps(p):
                act.wait_ge(bias_made, p + 1)
                for h in range(2):
                    nc.scalar.activation(probs[:, 256 * h:256 * h + 256], ps[:, SB0 + h, 0:256], ACT.Exp,
                                         bias=nbias[:, p, h:h + 1], scale=SCALE, accum_out=psums[:, p, h:h + 1])
                for h in range(2):
                    last = nc.scalar.activation(probs[:, 512 + 128 * h:640 + 128 * h], ps[:, SB0 + h, 256:384],
                                                ACT.Exp, bias=nbias[:, p, 2 + h:3 + h], scale=SCALE,
                                                accum_out=psums[:, p, 2 + h:3 + h])
                last.then_inc(exp_made, 1)

            def probs_out(p):
                act.wait_ge(p_tr, p + 1)
                if p:
                    act.wait_ge(pv_done, p)
                nc.scalar.copy(probs_t[:], ps[:, TB:TB + 2, :].rearrange("p b n -> p (b n)")[:, 0:768]).then_inc(pt_made, 1)

            for n in range(U_LOOP):
                high(n + AHEAD)
                if n == S_GLU:
                    for c in range(CC):
                        act.wait_ge(glu_tr, c + 1)
                        nc.scalar.activation(conv[:, c], ps[:, TB + c, T:2 * T], ACT.Sigmoid,
                                             bias=vec[:, V_BGLU + CC + c:V_BGLU + CC + c + 1]).then_inc(glu_sig, 1)
                if n == S_QT:
                    qk_out(0, TB)
                if n == S_KT:
                    qk_out(1, SB0)
                if n < U_ATTN and n % 2 == 1 and n // 2 < GA:
                    take(n // 2)
                if S_ATT + 1 <= n <= S_ATT + PAIRS:
                    probs_out(n - S_ATT - 1)
                if S_ATT <= n < S_ATT + PAIRS:
                    exps(n - S_ATT)
                if n == S_ATT + PAIRS - 1:
                    take(GA)
                if n < U_ATTN and n % 2 == 1 and n // 2 > GA:
                    take(n // 2)
                if n == S_OT:
                    act.wait_ge(o_tr, 1)
                    nc.scalar.copy(b_hi[:, 0:CC], chunks(TB)).then_inc(o_hi, 1)
                if n == S_LN:
                    act.wait_ge(ln_chain, 3)
                    nc.scalar.activation(root[:, 1], ln_var[:], ACT.Sqrt).then_inc(root_made, 1)
                if n == S_LN + 1:
                    for c in range(CC):
                        act.wait_ge(zn_tr, 1)
                        nc.scalar.activation(conv[:, c], chunks(SB0)[:, c], ACT.Sigmoid, bias=vec[:, V_LNB + c:V_LNB + c + 1],
                                             scale=vec[:, V_LNG + c:V_LNG + c + 1]).then_inc(silu_sig, 1)
                    act.wait_ge(silu_made, CC + 1)
                    nc.scalar.copy(b_hi[:, CC:2 * CC], silu_x).then_inc(cz_hi, 1)
                if n == U_CONV + 1:
                    act.wait_ge(m_tr, 1)
                    nc.scalar.copy(a_hi[:, 0:4], chunks(TB)).then_inc(m_hi, 1)
                if n == U_OUT:
                    act.wait_ge(m_tr, 2)
                    nc.scalar.copy(a_hi[:, 4:8], chunks(SB0)).then_inc(m_hi, 1)
                if n in (U_OUT + 3, U_FF):
                    half = 0 if n == U_OUT + 3 else 1
                    act.wait_ge(h_tr, half + 1)
                    for c in range(4):
                        k = 4 * half + c
                        nc.scalar.activation(b_hi[:, k], chunks(TB)[:, c], ACT.Copy,
                                             scale=vec[:, V_GFFN + k:V_GFFN + k + 1]).then_inc(h_hi, 1)
                if n == U_FF:
                    for t in range(TT):
                        nc.scalar.activation(nat[:, t], res[:, t], ACT.Square,
                                             accum_out=sq_sum[:, 1, t:t + 1]).then_inc(sq_made, 1)
                    act.wait_ge(ms_made, 2)
                    nc.scalar.activation(root[:, 2], ms[:, 1], ACT.Sqrt).then_inc(root_made, 1)

            def relu_out():
                for t in range(TT):
                    last = nc.scalar.activation(nat[:, t, 0:W], ps[:, SB0 + t], ACT.Relu, scale=rstd[:, 2, t:t + 1])
                last.then_inc(relu_made, 1)

            act.wait_ge(used, U_LOOP)
            act.wait_ge(rstd_made, 3)
            relu_out()
            act.wait_ge(f_tr, 1)
            nc.scalar.copy(a_hi[:, 0:4], chunks(TB)).then_inc(f_hi, 1)
            with act.Fori(0, FB - 1) as i:
                for j in range(4):
                    slot = (j + AHEAD) % SLOTS
                    act.wait_ge(raw_full[slot], i * 16 + 16 * ((U_LOOP + j + AHEAD) // SLOTS + 1))
                    act.wait_ge(used, i * 4 + (U_LOOP + j + AHEAD - SLOTS + 1))
                    nc.scalar.copy(w_hi[:, slot], raw[:, slot]).then_inc(hi_made, 1)
                    if j == 1:
                        act.wait_ge(used, i * 4 + (U_LOOP + 2))
                        act.wait_ge(sq_hidden, i + 1)
                        relu_out()
                    if j == 3:
                        act.wait_ge(f_tr, i + 2)
                        nc.scalar.copy(a_hi[:, 0:4], chunks(TB)).then_inc(f_hi, 1)
            for t in range(TT):
                for col in range(2):
                    act.wait_ge(y_made, 2 * t + col + 1)
                    nc.scalar.activation(nat[:, t, col * W:col * W + W], res[:, t, col * W:col * W + W], ACT.Square,
                                         accum_out=sq_sum[:, 2, 2 * t + col:2 * t + col + 1]).then_inc(sq_made, 1)
                act.wait_ge(ms_made, 3 + t)
                nc.scalar.activation(root[:, 3, t:t + 1], ms[:, 2, t:t + 1], ACT.Sqrt).then_inc(root_made, 1)

        @block.vector
        def _(dve):
            def low(n):
                if n in POOL_LO:
                    return
                dve.wait_ge(hi_made, n + 1)
                nc.vector.tensor_tensor(w_lo[:, n % SLOTS], raw[:, n % SLOTS], w_hi[:, n % SLOTS].bitcast(F32),
                                        ALU.subtract).then_inc(lo_made, 1)

            dve.wait_ge(vec_made, 1)
            for half in range(2):
                for c in range(4):
                    k = 4 * half + c
                    dve.wait_ge(xt_hi, k // 2 * 2 + 2)
                    nc.vector.scalar_tensor_tensor(out=a_lo[:, k], in0=chunks(TB if half == 0 else 2)[:, c],
                                                   scalar=vec[:, V_GMIX + k:V_GMIX + k + 1],
                                                   in1=a_hi[:, k].bitcast(F32), op0=ALU.mult,
                                                   op1=ALU.subtract).then_inc(xt_lo, 1)
                if half == 0:
                    low(0)
            dve.wait_ge(sq_made, TT)
            nc.vector.tensor_scalar(ms[:, 0], sq_sum[:, 0, 0:TT], 1.0 / D, EPS, ALU.mult, ALU.add).then_inc(ms_made, 1)
            low(1)
            dve.wait_ge(root_made, 1)
            nc.vector.reciprocal(rstd[:, 0], root[:, 0]).then_inc(rstd_made, 1)

            def conv_products(step):
                first, end = conv_share(step)
                for m in range(first, end):
                    tap, c = divmod(m, CC)
                    if tap == 0:
                        nc.vector.tensor_scalar(conv[:, c], z[:, c, 0:T], dw[:, c:c + 1], vec[:, V_BDW + c:V_BDW + c + 1],
                                                ALU.mult, ALU.add).then_inc(conv_step, 1)
                    else:
                        dve.wait_ge(conv_step, m - CC + 1)
                        nc.vector.scalar_tensor_tensor(out=conv[:, c], in0=z[:, c, tap:tap + T], scalar=dw[:, m:m + 1],
                                                       in1=conv[:, c], op0=ALU.mult, op1=ALU.add).then_inc(conv_step, 1)

            def row_max(p):
                dve.wait_ge(scored, p + 1)
                nc.vector.tensor_reduce(smax[:, p, 0:2], ps[:, SB0:SB0 + 2, 0:256], AX.X,
                                        ALU.max).then_inc(max_made, 1)
                nc.vector.tensor_reduce(smax[:, p, 2:4], ps[:, SB0:SB0 + 2, 256:384], AX.X,
                                        ALU.max).then_inc(max_made, 1)
                dve.wait_ge(max_made, 2 * p + 2)
                nc.vector.tensor_scalar(nbias[:, p], smax[:, p], -SCALE, None, ALU.mult).then_inc(bias_made, 1)

            def inverse(p):
                dve.wait_ge(exp_made, p + 1)
                nc.vector.reciprocal(rinv[:, p], psums[:, p]).then_inc(rinv_made, 1)

            def o_out(p):
                dve.wait_ge(pv_done, p + 1)
                dve.wait_ge(rinv_made, p + 1)
                for s in range(2):
                    last = nc.vector.tensor_tensor(
                        o_nat[:, 1 - s, 128 * p:128 * p + 128].rearrange("p (h d) -> p h d", h=2),
                        ps[:, SB0:SB0 + 2, 384 + HD * s:384 + HD * s + HD],
                        rinv[:, p, 2 * s:2 * s + 2].rearrange("p (h a) -> p h a", a=1).to_broadcast([P, 2, HD]), ALU.mult)
                last.then_inc(o_made, 1)

            for n in range(U_LOOP):
                low(n + AHEAD)
                conv_products(n)
                if n == S_GLU:
                    for c in range(CC):
                        dve.wait_ge(glu_sig, c + 1)
                        nc.vector.scalar_tensor_tensor(out=z[:, c, PAD:PAD + T], in0=ps[:, TB + c, 0:T],
                                                       scalar=vec[:, V_BGLU + c:V_BGLU + c + 1], in1=conv[:, c],
                                                       op0=ALU.add, op1=ALU.mult).then_inc(z_made, 1)
                    dve.wait_ge(z_made, CC)
                    dve.wait_ge(vec_made, 2)
                    dve.wait_ge(const_made, 4)
                if S_ATT + 2 <= n < S_ATT + 2 + PAIRS:
                    o_out(n - S_ATT - 2)
                if S_ATT + 1 <= n < S_ATT + 1 + PAIRS:
                    inverse(n - S_ATT - 1)
                if S_ATT <= n < S_ATT + PAIRS:
                    row_max(n - S_ATT)
                if n == S_OT:
                    dve.wait_ge(o_hi, 1)
                    nc.vector.tensor_tensor(b_lo[:, 0:CC], chunks(TB), b_hi[:, 0:CC].bitcast(F32),
                                            ALU.subtract).then_inc(o_lo, 1)
                if n == S_LN:
                    dve.wait_ge(conv_tr, 1)
                    for t in range(TT):
                        nc.vector.bn_stats(stats[:, t], ps[:, TB + t]).then_inc(ln_chain, 1)
                    dve.wait_ge(ln_chain, TT)
                    for t in range(TT):
                        last = nc.vector.bn_aggr(mean_var[:, t], stats[:, t])
                    last.then_inc(zn_made, 1)
                    dve.wait_ge(zn_made, 1)
                    nc.vector.tensor_scalar(ln_var[:], mean_var[:, :, 1], EPS, None, ALU.add).then_inc(ln_chain, 1)
                    dve.wait_ge(root_made, 2)
                    nc.vector.reciprocal(rstd[:, 1], root[:, 1]).then_inc(rstd_made, 1)
                    dve.wait_ge(rstd_made, 2)
                    for t in range(TT):
                        nc.vector.tensor_scalar(zn[:, t], ps[:, TB + t], mean_var[:, t, 0:1], rstd[:, 1, t:t + 1],
                                                ALU.subtract, ALU.mult).then_inc(zn_made, 1)
                if n == S_LN + 1:
                    dve.wait_ge(zn_tr, 1)
                    for c in range(CC):
                        dve.wait_ge(silu_sig, c // 2 * 2 + 2)
                        nc.vector.tensor_scalar(silu_x[:, c], chunks(SB0)[:, c], vec[:, V_LNG + c:V_LNG + c + 1],
                                                vec[:, V_LNB + c:V_LNB + c + 1], ALU.mult, ALU.add).then_inc(silu_made, 1)
                    dve.wait_ge(silu_made, CC)
                    nc.vector.tensor_tensor(silu_x, silu_x, conv[:], ALU.mult).then_inc(silu_made, 1)
                    dve.wait_ge(cz_hi, 1)
                    nc.vector.tensor_tensor(b_lo[:, CC:2 * CC], silu_x, b_hi[:, CC:2 * CC].bitcast(F32),
                                            ALU.subtract).then_inc(cz_lo, 1)
                if n in (U_ATTN, U_ATTN + 1):
                    col = n - U_ATTN
                    dve.wait_ge(used, n + 1)
                    dve.wait_ge(evac, len(ORDER))
                    for t in range(TT):
                        last = nc.vector.tensor_tensor(nat[:, t, col * W:col * W + W], ps[:, 2 * (1 - col) + t],
                                                       gates[:, 0, t, col * W:col * W + W], ALU.mult)
                    last.then_inc(m_attn, 1)
                if n in (U_CONV, U_CONV + 1):
                    col = n - U_CONV
                    dve.wait_ge(used, n + 1)
                    dve.wait_ge(m_bias, col + 1)
                    for t in range(TT):
                        g = gates[:, 1, t, col * W:col * W + W]
                        nc.vector.tensor_tensor(g, ps[:, 2 * (1 - col) + t], g, ALU.mult).then_inc(m_conv, 1)
                    for t in range(TT):
                        dve.wait_ge(m_conv, 2 * col + t + 1)
                        part = nat[:, t, col * W:col * W + W]
                        nc.vector.tensor_tensor(part, part, gates[:, 1, t, col * W:col * W + W], ALU.add).then_inc(merged, 1)
                if n == U_CONV + 1:
                    dve.wait_ge(m_hi, 1)
                    nc.vector.tensor_tensor(a_lo[:, 0:4], chunks(TB), a_hi[:, 0:4].bitcast(F32),
                                            ALU.subtract).then_inc(m_lo, 1)
                if n == U_OUT:
                    dve.wait_ge(m_hi, 2)
                    nc.vector.tensor_tensor(a_lo[:, 4:8], chunks(SB0), a_hi[:, 4:8].bitcast(F32),
                                            ALU.subtract).then_inc(m_lo, 1)
                if n in (U_OUT + 2, U_OUT + 3):
                    col = n - U_OUT - 2
                    dve.wait_ge(used, n + 1)
                    for t in range(TT):
                        part = res[:, t, col * W:col * W + W]
                        nc.vector.tensor_tensor(part, ps[:, 2 * (1 - col) + t], part, ALU.add).then_inc(res2, 1)
                if n in (U_OUT + 3, U_FF):
                    half = 0 if n == U_OUT + 3 else 1
                    for c in range(4):
                        k = 4 * half + c
                        dve.wait_ge(h_hi, k // 2 * 2 + 2)
                        nc.vector.scalar_tensor_tensor(out=b_lo[:, k], in0=chunks(TB)[:, c],
                                                       scalar=vec[:, V_GFFN + k:V_GFFN + k + 1],
                                                       in1=b_hi[:, k].bitcast(F32), op0=ALU.mult,
                                                       op1=ALU.subtract).then_inc(h_lo, 1)
                if n == U_FF:
                    dve.wait_ge(sq_made, 2 * TT)
                    nc.vector.tensor_scalar(ms[:, 1], sq_sum[:, 1, 0:TT], 1.0 / D, EPS, ALU.mult, ALU.add).then_inc(ms_made, 1)
                    dve.wait_ge(root_made, 3)
                    nc.vector.reciprocal(rstd[:, 2], root[:, 2]).then_inc(rstd_made, 1)

            def hidden_low():
                nc.vector.tensor_tensor(a_lo[:, 0:4], chunks(TB), a_hi[:, 0:4].bitcast(F32), ALU.subtract).then_inc(f_lo, 1)

            dve.wait_ge(f_hi, 1)
            hidden_low()
            with dve.Fori(0, FB - 1) as i:
                for j in range(4):
                    slot = (j + AHEAD) % SLOTS
                    dve.wait_ge(hi_made, i * 4 + (U_LOOP + j + AHEAD + 1))
                    nc.vector.tensor_tensor(w_lo[:, slot], raw[:, slot], w_hi[:, slot].bitcast(F32),
                                            ALU.subtract).then_inc(lo_made, 1)
                dve.wait_ge(f_hi, i + 2)
                hidden_low()
            for t in range(TT):
                dve.wait_ge(ff_done, t + 1)
                for col in range(2):
                    part = res[:, t, col * W:col * W + W]
                    nc.vector.tensor_tensor(part, ps[:, 2 * t + col], part, ALU.add).then_inc(y_made, 1)
                dve.wait_ge(sq_made, 2 * TT + 2 * t + 2)
                nc.vector.tensor_reduce(sq_sum[:, 1, t:t + 1], sq_sum[:, 2, 2 * t:2 * t + 2], AX.X, ALU.add).then_inc(max_made, 1)
                dve.wait_ge(max_made, 2 * PAIRS + t + 1)
                nc.vector.tensor_scalar(ms[:, 2, t:t + 1], sq_sum[:, 1, t:t + 1], 1.0 / D, EPS, ALU.mult,
                                        ALU.add).then_inc(ms_made, 1)
                dve.wait_ge(root_made, 4 + t)
                nc.vector.reciprocal(rstd[:, 3, t:t + 1], root[:, 3, t:t + 1]).then_inc(rstd_made, 1)
                dve.wait_ge(rstd_made, 4 + t)
                if t == 0:
                    dve.wait_ge(bc_full, 32)
                nc.vector.scalar_tensor_tensor(out=res[:, t], in0=res[:, t], scalar=rstd[:, 3, t:t + 1], in1=gfin_bc[:],
                                               op0=ALU.mult, op1=ALU.mult).then_inc(out_made, 1)

        @block.tensor
        def _(pe):
            def transpose(dst, src):
                return nc.tensor.transpose(dst, src, ident[0:src.shape[0], 0:src.shape[0]])

            def transpose_chunks(bank, source):
                for c in range(4):
                    for t in range(TT):
                        last = transpose(chunks(bank)[:, c, t * P:t * P + P], source(t, c))
                return last

            def products(slot, k, hi, lo, bank, t, start, stop):
                dst = ps[:, bank]
                tok = slice(t * P, t * P + P)
                nc.tensor.matmul(dst, hi[:, tok], w_hi[:, slot, k], start=start, stop=False)
                nc.tensor.matmul(dst, lo[:, tok], w_hi[:, slot, k], start=False, stop=False)
                return nc.tensor.matmul(dst, hi[:, tok], w_lo[:, slot, k], start=False, stop=stop)

            def weights(n):
                dve, pool = low_count(n)
                pe.wait_ge(hi_made, n + 1)
                pe.wait_ge(lo_made, dve)
                if pool:
                    pe.wait_ge(lo_made_pool, pool)

            def unit(n, hi, lo, first, bank, start, stop, between=None):
                weights(n)
                for t in range(TT):
                    for k in range(HK):
                        last = products(n % SLOTS, k, hi[:, first + k], lo[:, first + k], bank(t), t,
                                        start and k == 0, stop and k == HK - 1)
                    if t == 0 and between is not None:
                        between()
                last.then_inc(used, 1)

            pe.wait_ge(ident_made, 1)
            pe.wait_ge(vec_full, 16 * 7)
            transpose(ps[:, TB, 0:VROWS], vec_rows[:])
            transpose(ps[:, TB, P:P + TAPS * CC], dw_rows[:]).then_inc(vec_tr, 1)
            pe.wait_ge(x_full, 16 * TT)
            transpose_chunks(2, lambda t, c: res[:, t, (4 + c) * P:(5 + c) * P])
            pe.wait_ge(vec_made, 2)
            transpose_chunks(TB, lambda t, c: res[:, t, c * P:c * P + P]).then_inc(x_tr, 2)

            def scores(p):
                if p >= 2:
                    pe.wait_ge(o_made, p - 1)
                for s, at, keys in ((1, 0, 256), (0, 256, 128)):
                    for h in range(2):
                        rows = slice(HD * h, HD * h + HD)
                        nc.tensor.matmul(ps[:, SB0 + h, at:at + keys], qk_t[rows, 0, p, s * P:s * P + P],
                                         qk_t[rows, 1, p, 0:keys], start=True, stop=False)
                    for h in range(2):
                        last = nc.tensor.matmul(ps[:, SB0 + h, at:at + keys], ident_b[:], mask_b[:, T - keys:T],
                                                start=False, stop=True)
                last.then_inc(scored, 1)

            def probs_transposed(p):
                pe.wait_ge(exp_made, p + 1)
                if p:
                    pe.wait_ge(pt_made, p)
                for blk in range(6):
                    o = blk * P
                    last = transpose(ps[:, TB + o // W, o % W:o % W + P], probs[:, o:o + P])
                last.then_inc(p_tr, 1)

            def values(p):
                pe.wait_ge(pt_made, p + 1)
                if p:
                    pe.wait_ge(o_made, p)
                if p + 2 <= PAIRS:
                    pe.wait_ge(exp_made, p + 2)
                for s in range(2):
                    for h in range(2):
                        head = slice(HD * (2 * p + h), HD * (2 * p + h) + HD)
                        o = 384 + HD * s
                        n_keys = 2 - s
                        for kb in range(n_keys):
                            at = 256 * h + P * kb if s == 0 else 512 + P * h
                            last = nc.tensor.matmul(ps[:, SB0 + h, o:o + HD], probs_t[:, at:at + P], v_nat[:, kb, head],
                                                    start=kb == 0, stop=kb == n_keys - 1)
                last.then_inc(pv_done, 1)

            for n in range(U_ATTN):
                b, half = divmod(n, 2)
                if n == 0:
                    pe.wait_ge(xt_lo, 4)
                if n == 1:
                    pe.wait_ge(xt_lo, 8)
                if half == 0 and b >= 2:
                    pe.wait_ge(evac, b - 1)
                unit(n, a_hi, a_lo, HK * half, lambda t: 2 * (b % 2) + t, half == 0, half == 1)
                if n == S_GLU:
                    pe.wait_ge(evac, UG + 1)
                    for c in range(CC):
                        for part in range(2):
                            for t in range(TT):
                                last = transpose(ps[:, TB + c, part * T + t * P:part * T + t * P + P],
                                                 nat[:, t, part * W + c * P:part * W + c * P + P])
                        last.then_inc(glu_tr, 1)
                if n == S_QT:
                    pe.wait_ge(evac, Q + 1)
                    pe.wait_ge(z_made, CC)
                    transpose_chunks(TB, lambda t, c: nat[:, t, c * P:c * P + P]).then_inc(qk_tr, 1)
                if n == S_KT:
                    pe.wait_ge(evac, K + 1)
                    transpose_chunks(SB0, lambda t, c: nat[:, t, W + c * P:W + c * P + P]).then_inc(qk_tr, 1)
                if S_ATT + 2 <= n < S_ATT + 2 + PAIRS:
                    if n == S_ATT + 2:
                        pe.wait_ge(evac, V + 1)
                    values(n - S_ATT - 2)
                if S_ATT + 1 <= n <= S_ATT + PAIRS:
                    probs_transposed(n - S_ATT - 1)
                if S_ATT <= n < S_ATT + PAIRS:
                    if n == S_ATT:
                        pe.wait_ge(qk_made, 2)
                        pe.wait_ge(ident_made, 3)
                    scores(n - S_ATT)
                if n == S_OT:
                    pe.wait_ge(o_made, PAIRS)
                    transpose_chunks(TB, lambda t, c: o_nat[:, t, c * P:c * P + P]).then_inc(o_tr, 1)
                if n == S_LN:
                    pe.wait_ge(conv_step, TAPS * CC)
                    pe.wait_ge(o_lo, 1)
                    for t in range(TT):
                        for c in range(CC):
                            last = transpose(ps[:, TB + t, c * P:c * P + P], conv[:, c, t * P:t * P + P])
                    last.then_inc(conv_tr, 1)

            def zn_back():
                pe.wait_ge(zn_made, 1 + TT)
                transpose_chunks(SB0, lambda t, c: zn[:, t, c * P:c * P + P]).then_inc(zn_tr, 1)

            def merged_transposed(col, bank):
                pe.wait_ge(merged, 2 * col + 2)
                transpose_chunks(bank, lambda t, c: nat[:, t, col * W + c * P:col * W + c * P + P]).then_inc(m_tr, 1)

            def res_transposed(col):
                pe.wait_ge(res2, 2 * col + 2)
                transpose_chunks(TB, lambda t, c: res[:, t, col * W + c * P:col * W + c * P + P]).then_inc(h_tr, 1)

            for col in range(2):
                pe.wait_ge(o_lo, 1)
                pe.wait_ge(evac, len(ORDER) - 1 + col)
                unit(U_ATTN + col, b_hi, b_lo, 0, lambda t: 2 * (1 - col) + t, True, True)
                if col == 0:
                    zn_back()
            for col in range(2):
                pe.wait_ge(cz_lo, 1)
                pe.wait_ge(m_attn, col + 1)
                unit(U_CONV + col, b_hi, b_lo, CC, lambda t: 2 * (1 - col) + t, True, True,
                     (lambda: merged_transposed(0, TB)) if col == 1 else None)
            for half in range(2):
                for col in range(2):
                    if half == 0:
                        pe.wait_ge(m_lo, 1)
                        pe.wait_ge(merged, 2 * col + 2)
                    else:
                        pe.wait_ge(m_lo, 2)
                    unit(U_OUT + 2 * half + col, a_hi, a_lo, HK * half, lambda t: 2 * (1 - col) + t, half == 0, half == 1,
                         (lambda: res_transposed(0)) if half == 1 and col == 1 else None)
                    if half == 0 and col == 0:
                        merged_transposed(1, SB0)
            for half in range(2):
                pe.wait_ge(h_lo, 4 * half + 4)
                def second():
                    pe.wait_ge(h_lo, 4)
                    res_transposed(1)
                unit(U_FF + half, b_hi, b_lo, HK * half, lambda t: SB0 + t, half == 0, half == 1,
                     second if half == 0 else None)

            def hidden_transposed():
                return transpose_chunks(TB, lambda t, c: nat[:, t, W + c * P:W + c * P + P])

            for bank in range(4):
                nc.tensor.matmul(ps[:, bank], zero_b[:, 0:P], zero_b[:], start=True, stop=False)
            pe.wait_ge(sq_hidden, 1)
            hidden_transposed().then_inc(f_tr, 1)

            pools = len(POOL_LO)
            with pe.Fori(0, FB - 1) as i:
                for j in range(4):
                    pe.wait_ge(hi_made, i * 4 + (U_LOOP + j + 1))
                    pe.wait_ge(lo_made, i * 4 + (U_LOOP + j + 1 - pools))
                    if j == 0:
                        pe.wait_ge(relu_made, i + 1)
                    if j == 2:
                        pe.wait_ge(f_lo, i + 1)
                    for t in range(TT):
                        for k in range(HK):
                            if j < 2:
                                last = products(j, k, b_hi[:, HK * j + k], b_lo[:, HK * j + k], SB0 + t, t,
                                                j == 0 and k == 0, j == 1 and k == HK - 1)
                            else:
                                last = products(j, k, a_hi[:, k], a_lo[:, k], 2 * t + j - 2, t, False, False)
                    last.then_inc(used, 1)
                pe.wait_ge(sq_hidden, i + 2)
                hidden_transposed().then_inc(f_tr, 1)
            pe.wait_ge(f_lo, FB)
            weights(U_LAST + 1)
            for t in range(TT):
                for col in range(2):
                    for k in range(HK):
                        last = products(col, k, a_hi[:, k], a_lo[:, k], 2 * t + col, t, False, k == HK - 1)
                last.then_inc(ff_done, 1)


_INS = ['x', 'g_mix', 'w_in', 'b_glu', 'w_dw', 'b_dw', 'ln_g', 'ln_b', 'w_conv_pw', 'b_conv_pw',
        'w_attn_up', 'w_out', 'g_ffn', 'w_ff1', 'w_ff2', 'g_final']
_OUTS = [((1, 256, 1024), 'float32')]


def kernel(**inputs):
    import numpy as _np
    import concourse.bacc as _bacc
    from concourse import mybir as _mybir
    from concourse.bass_utils import run_bass_kernel_spmd as _run

    nc = _bacc.Bacc("TRN2", target_bir_lowering=False, num_devices=1)
    arrays, args = {}, []
    for name in _INS:
        a = _np.ascontiguousarray(inputs[name])
        arrays[f"in_{name}_dram"] = a
        args.append(nc.dram_tensor(f"in_{name}_dram", a.shape, _mybir.dt.from_np(a.dtype), kind="ExternalInput").ap())
    for i, (shape, dtype) in enumerate(_OUTS):
        dt = _mybir.dt.from_np(_np.dtype(dtype))
        args.append(nc.dram_tensor(f"out_{i}_dram", shape, dt, kind="ExternalOutput").ap())
    build(nc, *args)
    r = _run(nc, [arrays], core_ids=[0])
    got = tuple(r.results[0][f"out_{i}_dram"] for i in range(len(_OUTS)))
    return got[0]
```

```python
from contextlib import ExitStack

import concourse.bass as bass
from concourse import mybir

P = 128
T = 256
TT = T // P
D = 1024
KD = D // P
HEADS, HD = 8, 64
A = HEADS * HD
C = D // 2
CC = C // P
TAPS = 31
F = 4 * D
W = 512
HK = 4
EPS = 1e-6
SCALE = HD ** -0.5
MASKED = -1e30

SLOTS = 4
WARM = 9
AHEAD = 2

ORDER = [3, 4, 0, 1, 2, 5, 6, 7, 8]
UG, Q, K, V, GA, GC = 1, 2, 3, 4, 5, 7
U_ATTN = 2 * len(ORDER)
U_CONV = U_ATTN + 2
U_OUT = U_CONV + 2
U_FF = U_OUT + 4
FB = F // W
U_LOOP = U_FF + 2
U_LAST = U_LOOP + 4 * (FB - 1)
UNITS = U_LAST + 2
assert U_LOOP % SLOTS == 0

S_VEC = 2
S_GLU = 4
S_QT, S_KT = 6, 8
S_ATT = 9
PAIRS = HEADS // 2
S_OT = S_ATT + 6
S_LN = 16
TAPS_AT = {5: 15, 6: 15, 7: 15, 8: 15, 9: 11, 10: 10, 11: 9, 12: 10, 13: 11, 14: 13}
assert sum(TAPS_AT.values()) == TAPS * 4
POOL_LO = (6, 7, 9, 10, 12, 14, 16, 22, 24)
assert max(POOL_LO) <= U_LOOP - SLOTS

F32 = mybir.dt.float32
F32R = mybir.dt.float32r
BF16 = mybir.dt.bfloat16
ALU = mybir.AluOpType
ACT = mybir.ActivationFunctionType
AX = mybir.AxisListType

V_BGLU, V_BDW, V_LNG, V_LNB, V_GFFN = 0, 8, 12, 16, 20
VROWS = 28


def conv_share(step):
    first = sum(TAPS_AT[m] for m in TAPS_AT if m < step)
    return range(first, first + TAPS_AT.get(step, 0))


def low_count(n):
    pool = sum(1 for u in POOL_LO if u <= n)
    return n + 1 - pool, pool


def build(nc, x, g_mix, w_in, b_glu, w_dw, b_dw, ln_g, ln_b, w_conv_pw, b_conv_pw,
          w_attn_up, w_out, g_ffn, w_ff1, w_ff2, g_final, out):
    x_v = x.rearrange("b (t p) d -> p (b t) d", p=P)
    out_v = out.rearrange("b (t p) d -> p (b t) d", p=P)
    win_v = w_in.rearrange("l (c p) n -> p (l c) n", p=P)
    wattn_v = w_attn_up.rearrange("l (c p) n -> p (l c) n", p=P)
    wconv_v = w_conv_pw.rearrange("l (c p) n -> p (l c) n", p=P)
    wout_v = w_out.rearrange("l (c p) n -> p (l c) n", p=P)
    wff1_v = w_ff1.rearrange("l (c p) n -> p (l c) n", p=P)
    wff2_v = w_ff2.rearrange("l (f c p) n -> (l f) p c n", p=P, c=HK)

    def unit_source(n):
        if n < U_ATTN:
            b, half = divmod(n, 2)
            return win_v[:, HK * half:HK * half + HK, ORDER[b] * W:ORDER[b] * W + W]
        if n < U_OUT:
            v = wattn_v if n < U_CONV else wconv_v
            col = (n - U_ATTN) % 2
            return v[:, :, col * W:col * W + W]
        if n < U_FF:
            half, col = divmod(n - U_OUT, 2)
            return wout_v[:, HK * half:HK * half + HK, col * W:col * W + W]
        return wff1_v[:, HK * (n - U_FF):HK * (n - U_FF) + HK, 0:W]

    with ExitStack() as ctx:
        def sb(name, shape, dt=F32):
            return ctx.enter_context(nc.sbuf_tensor(name, shape, dt))

        def sem(name):
            return ctx.enter_context(nc.semaphore(name))

        raw = sb("raw", [P, SLOTS, HK, W])
        w_hi = sb("w_hi", [P, SLOTS, HK, W], F32R)
        w_lo = sb("w_lo", [P, SLOTS, HK, W], F32R)
        a_hi = sb("a_hi", [P, KD, T], F32R)
        a_lo = sb("a_lo", [P, KD, T], F32R)
        b_hi = sb("b_hi", [P, KD, T], F32R)
        b_lo = sb("b_lo", [P, KD, T], F32R)
        res = sb("res", [P, TT, D])
        nat = sb("nat", [P, TT, D])
        gates = sb("gates", [P, 2, TT, D])
        v_nat = sb("v_nat", [P, TT, A])
        qk_t = sb("qk_t", [P, 2, CC, T])
        probs = sb("probs", [P, 768])
        probs_t = sb("probs_t", [P, 768])
        o_nat = sb("o_nat", [P, TT, A])
        PAD = TAPS - 1
        z = sb("z", [P, CC, PAD + T])
        conv = sb("conv", [P, CC, T])
        zn = sb("zn", [P, TT, C])
        gmix_rows = sb("gmix_rows", [KD, P])
        gmix = sb("gmix", [P, KD])
        vec_rows = sb("vec_rows", [VROWS, P])
        dw_rows = sb("dw_rows", [TAPS * CC, P])
        vec = sb("vec", [P, VROWS])
        dw = sb("dw", [P, TAPS * CC])
        gfin_bc = sb("gfin_bc", [P, D])
        bpw_bc = sb("bpw_bc", [P, D])
        ident = sb("ident", [P, P])
        ident_b = sb("ident_b", [P, P], BF16)
        mask_b = sb("mask_b", [P, T], BF16)
        zero_b = sb("zero_b", [P, W], BF16)
        first_sig = sb("first_sig", [P, 1])
        sq_sum = sb("sq_sum", [P, 3, 4])
        ms = sb("ms", [P, 3, TT])
        half_neg = sb("half_neg", [P, TT])
        rstd = sb("rstd", [P, 3 + TT, TT])
        stats = sb("stats", [P, TT, 6])
        mean_var = sb("mean_var", [P, TT, 2])
        ln_var = sb("ln_var", [P, TT])
        smax = sb("smax", [P, PAIRS, 4])
        nbias = sb("nbias", [P, PAIRS, 4])
        psums = sb("psums", [P, PAIRS, 4])
        rinv = sb("rinv", [P, PAIRS, 4])
        silu_x = zn[:, :, :].rearrange("p t c -> p (t c)").rearrange("p (c t) -> p c t", c=CC)
        gcb = qk_t[:, :, :, :].rearrange("p a c t -> p (a c t)").rearrange("p (t d) -> p t d", t=TT)

        ps = ctx.enter_context(nc.psum_tensor("ps", [P, 8, W], F32))
        TB, SB0 = 4, 6

        def x_chunk(k):
            bank = (4, 5, 2, 3)[k // 2]
            return ps[:, bank, k % 2 * T:k % 2 * T + T]

        def tile_chunks(bank, t):
            return ps[:, bank + t, :].rearrange("p (c t) -> p c t", c=4)

        def chunks(bank):
            return ps[:, bank:bank + 2, :].rearrange("p b n -> p (b n)").rearrange("p (c t) -> p c t", c=4)

        raw_full = [sem(f"raw_full{i}") for i in range(SLOTS)]
        x_full = [sem(f"x_full{t}") for t in range(TT)]
        first_full = sem("first_full")
        first_hi = sem("first_hi")
        first_lo = sem("first_lo")
        gmix_full = sem("gmix_full")
        gmix_tr = sem("gmix_tr")
        gmix_made = sem("gmix_made")
        zero_made = sem("zero_made")
        tile_done = sem("tile_done")
        vec_full = sem("vec_full")
        bc_full = sem("bc_full")
        hi_made = sem("hi_made")
        lo_made = sem("lo_made")
        lo_made_pool = sem("lo_made_pool")
        used = sem("used")
        const_made = sem("const_made")
        ident_made = sem("ident_made")
        vec_tr = sem("vec_tr")
        vec_made = sem("vec_made")
        x_tr = sem("x_tr")
        xt_hi = sem("xt_hi")
        xt_lo = sem("xt_lo")
        sq_made = sem("sq_made")
        ms_made = sem("ms_made")
        rstd_made = sem("rstd_made")
        evac = sem("evac")
        glu_tr = sem("glu_tr")
        glu_sig = sem("glu_sig")
        z_made = sem("z_made")
        conv_step = sem("conv_step")
        conv_tr = sem("conv_tr")
        ln_chain = sem("ln_chain")
        zn_made = sem("zn_made")
        zn_tr = sem("zn_tr")
        silu_sig = sem("silu_sig")
        silu_made = sem("silu_made")
        cz_hi = sem("cz_hi")
        cz_lo = sem("cz_lo")
        qk_tr = sem("qk_tr")
        qk_made = sem("qk_made")
        scored = sem("scored")
        max_made = sem("max_made")
        bias_made = sem("bias_made")
        exp_made = sem("exp_made")
        p_tr = sem("p_tr")
        pt_made = sem("pt_made")
        pv_done = sem("pv_done")
        rinv_made = sem("rinv_made")
        o_made = sem("o_made")
        o_tr = sem("o_tr")
        o_hi = sem("o_hi")
        o_lo = sem("o_lo")
        gcb_made = sem("gcb_made")
        m_attn = sem("m_attn")
        m_bias = sem("m_bias")
        m_conv = sem("m_conv")
        merged = sem("merged")
        m_tr = sem("m_tr")
        m_hi = sem("m_hi")
        m_lo = sem("m_lo")
        res2 = sem("res2")
        h_tr = sem("h_tr")
        h_hi = sem("h_hi")
        h_lo = sem("h_lo")
        relu_made = sem("relu_made")
        sq_hidden = sem("sq_hidden")
        f_tr = sem("f_tr")
        f_hi = sem("f_hi")
        f_lo = sem("f_lo")
        ff_done = sem("ff_done")
        y_made = sem("y_made")
        out_made = sem("out_made")
        out_made_act = sem("out_made_act")
        mean_part = sem("mean_part")
        y_scaled = sem("y_scaled")
        stored = sem("stored")

        block = ctx.enter_context(nc.Block())

        @block.sync
        def _(sp):
            def load(n, source, part=slice(0, HK)):
                if n >= SLOTS:
                    dve, pool = low_count(n - SLOTS)
                    sp.wait_ge(lo_made, dve)
                    if pool:
                        sp.wait_ge(lo_made_pool, pool)
                sp.dma_start(raw[:, n % SLOTS, part], source).then_inc(raw_full[n % SLOTS], 16)

            for t in range(TT):
                sp.dma_start(res[:, t], x_v[:, t]).then_inc(x_full[t], 16)
            first = unit_source(0)
            sp.dma_start(raw[:, 0, 0:2], first[:, 0:2]).then_inc(first_full, 16)
            load(0, first[:, 2:HK], slice(2, HK))
            for n in range(1, U_LOOP):
                load(n, unit_source(n))
                if n == 1:
                    for row, v in ((V_BGLU, b_glu), (V_BDW, b_dw), (V_LNG, ln_g), (V_LNB, ln_b), (V_GFFN, g_ffn)):
                        rows = v.shape[1] // P
                        sp.dma_start(vec_rows[row:row + rows, :], v.rearrange("l (c p) -> (l c) p", p=P)).then_inc(vec_full, 16)
                    sp.dma_start(dw_rows[:], w_dw.rearrange("l j (c p) -> (l j c) p", p=P)).then_inc(vec_full, 16)
                if n == 8:
                    sp.dma_start(bpw_bc[:], b_conv_pw.to_broadcast([P, D])).then_inc(bc_full, 16)
                    sp.dma_start(gfin_bc[:], g_final.rearrange("(a d) -> a d", a=1).to_broadcast([P, D])).then_inc(bc_full, 16)
            pools = len(POOL_LO)
            sp.wait_ge(lo_made_pool, pools)
            with sp.Fori(0, FB - 1) as i:
                for j in range(4):
                    if j < 2:
                        source = wff1_v[:, HK * j:HK * j + HK, bass.ds(i * W + W, W)]
                    else:
                        source = wff2_v[bass.ds(i, 1), :, :, (j - 2) * W:(j - 1) * W].rearrange("f p c n -> p (f c) n")
                    sp.wait_ge(lo_made, i * 4 + (U_LOOP + j - SLOTS + 1 - pools))
                    sp.dma_start(raw[:, j], source).then_inc(raw_full[j], 16)
            for j in range(2):
                load(U_LAST + j, wff2_v[FB - 1, :, :, j * W:j * W + W])
            for t in range(TT):
                sp.wait_ge(out_made, t + 1)
                sp.dma_start(out_v[:, t, 0:W], res[:, t, 0:W]).then_inc(stored, 16)
            sp.wait_ge(stored, 32 * TT)

        @block.gpsimd
        def _(pool):
            nc.gpsimd.memset(ident[:], 0.0).then_inc(const_made, 1)
            pool.wait_ge(const_made, 1)
            nc.gpsimd.affine_select(out=ident[:], in_=ident[:], compare_op=ALU.not_equal, fill=1.0, base=0,
                                    pattern=[[-1, P]], channel_multiplier=1).then_inc(ident_made, 1)
            nc.gpsimd.memset(mask_b[:], 0.0).then_inc(const_made, 1)
            nc.gpsimd.memset(half_neg[:], -0.5).then_inc(const_made, 1)
            nc.gpsimd.memset(z[:, :, 0:PAD], 0.0).then_inc(const_made, 1)
            pool.wait_ge(const_made, 2)
            nc.gpsimd.affine_select(out=mask_b[:], in_=mask_b[:], compare_op=ALU.is_ge, fill=MASKED, base=P,
                                    pattern=[[-1, T]], channel_multiplier=1).then_inc(ident_made, 1)
            pool.wait_ge(ident_made, 1)
            nc.gpsimd.tensor_copy(ident_b[:], ident[:]).then_inc(ident_made, 1)
            pool.wait_ge(const_made, 3)

            def inverse_root(k, source, count):
                pool.wait_ge(ms_made, count)
                n = source.shape[1]
                nc.gpsimd.tensor_tensor(rstd[:, k, 0:n], source, half_neg[:, 0:n], ALU.pow).then_inc(rstd_made, 1)

            inverse_root(0, ms[:, 0], 1)

            def low(n):
                pool.wait_ge(hi_made, n + 1)
                nc.gpsimd.tensor_tensor(w_lo[:, n % SLOTS], raw[:, n % SLOTS], w_hi[:, n % SLOTS].bitcast(F32),
                                        ALU.subtract).then_inc(lo_made_pool, 1)

            for n in POOL_LO:
                if n < U_ATTN:
                    low(n)
            pool.wait_ge(bc_full, 32)
            pool.wait_ge(scored, PAIRS)
            pool.wait_ge(evac, len(ORDER) - 1)
            for col in range(2):
                if col:
                    inverse_root(1, ln_var[:], 2)
                    pool.wait_ge(evac, len(ORDER))
                part = slice(col * W, col * W + W)
                nc.gpsimd.tensor_tensor(gcb[:, :, part], gates[:, 1, :, part],
                                        bpw_bc[:, part].rearrange("p (a n) -> p a n", a=1).to_broadcast([P, TT, W]),
                                        ALU.mult).then_inc(gcb_made, 1)
            for col in range(2):
                if 18 + col in POOL_LO:
                    low(18 + col)
                pool.wait_ge(m_attn, col + 1)
                pool.wait_ge(gcb_made, 2)
                part = nat[:, :, col * W:col * W + W]
                nc.gpsimd.tensor_tensor(part, part, gcb[:, :, col * W:col * W + W], ALU.add).then_inc(m_bias, 1)
            for n in POOL_LO:
                if n > U_ATTN + 1:
                    low(n)
            inverse_root(2, ms[:, 1], 3)
            pool.wait_ge(relu_made, 1)
            nc.gpsimd.tensor_tensor(nat[:, :, W:D], nat[:, :, 0:W], nat[:, :, 0:W], ALU.mult).then_inc(sq_hidden, 1)
            with pool.Fori(1, FB) as i:
                pool.wait_ge(relu_made, i + 1)
                pool.wait_ge(f_tr, i * 2)
                nc.gpsimd.tensor_tensor(nat[:, :, W:D], nat[:, :, 0:W], nat[:, :, 0:W], ALU.mult).then_inc(sq_hidden, 1)
            for t in range(TT):
                inverse_root(3 + t, ms[:, 2, t:t + 1], 4 + t)

        @block.scalar
        def _(act):
            act.dma_start(gmix_rows[:], g_mix.rearrange("l (c p) -> (l c) p", p=P)).then_inc(gmix_full, 16)

            def high(n):
                act.wait_ge(raw_full[n % SLOTS], 16 * (n // SLOTS + 1))
                if n >= SLOTS:
                    act.wait_ge(used, n - SLOTS + 1)
                part = slice(0, HK) if n else slice(2, HK)
                nc.scalar.copy(w_hi[:, n % SLOTS, part], raw[:, n % SLOTS, part]).then_inc(hi_made, 1)

            act.wait_ge(zero_made, 1)
            nc.scalar.activation(first_sig[:], zero_b[:, 0:1], ACT.Sigmoid)
            act.wait_ge(gmix_tr, 1)
            nc.scalar.copy(gmix[:], ps[:, SB0, 0:KD]).then_inc(gmix_made, 1)
            act.wait_ge(gmix_made, 1)
            for pair in range(4):
                act.wait_ge(x_tr, pair + 1)
                for k in (2 * pair, 2 * pair + 1):
                    nc.scalar.activation(a_hi[:, k], x_chunk(k), ACT.Copy, scale=gmix[:, k:k + 1]).then_inc(xt_hi, 1)
                if pair == 1:
                    high(0)
            high(1)
            for t in range(TT):
                nc.scalar.activation(nat[:, t], res[:, t], ACT.Square, accum_out=sq_sum[:, 0, t:t + 1]).then_inc(sq_made, 1)

            def take(b):
                bank = 2 * (b % 2)
                act.wait_ge(used, 2 * b + 2)
                if b == 0:
                    act.wait_ge(rstd_made, 1)
                if b == Q:
                    act.wait_ge(glu_tr, CC)
                if b < 2 or b in (Q, K):
                    dst, fn = nat[:, :, (b % 2) * W:(b % 2) * W + W], ACT.Copy
                elif b == V:
                    dst, fn = v_nat[:], ACT.Copy
                else:
                    g, col = divmod(b - GA, 2)
                    dst, fn = gates[:, g, :, col * W:col * W + W], ACT.Sigmoid
                for t in range(TT):
                    last = nc.scalar.activation(dst[:, t], ps[:, bank + t], fn, scale=rstd[:, 0, t:t + 1])
                last.then_inc(evac, 1)

            def qk_out(i, bank):
                act.wait_ge(qk_tr, i + 1)
                nc.scalar.copy(qk_t[:, i], chunks(bank)).then_inc(qk_made, 1)

            def exps(p):
                act.wait_ge(bias_made, p + 1)
                for h in range(2):
                    nc.scalar.activation(probs[:, 256 * h:256 * h + 256], ps[:, SB0 + h, 0:256], ACT.Exp,
                                         bias=nbias[:, p, h:h + 1], scale=SCALE, accum_out=psums[:, p, h:h + 1])
                for h in range(2):
                    last = nc.scalar.activation(probs[:, 512 + 128 * h:640 + 128 * h], ps[:, SB0 + h, 256:384],
                                                ACT.Exp, bias=nbias[:, p, 2 + h:3 + h], scale=SCALE,
                                                accum_out=psums[:, p, 2 + h:3 + h])
                last.then_inc(exp_made, 1)

            def probs_out(p):
                act.wait_ge(p_tr, p + 1)
                if p:
                    act.wait_ge(pv_done, p)
                nc.scalar.copy(probs_t[:], ps[:, TB:TB + 2, :].rearrange("p b n -> p (b n)")[:, 0:768]).then_inc(pt_made, 1)

            for n in range(U_LOOP):
                high(n + AHEAD)
                if n == S_VEC:
                    act.wait_ge(vec_tr, 1)
                    nc.scalar.copy(vec[:], ps[:, SB0 + 1, 0:VROWS]).then_inc(vec_made, 1)
                    nc.scalar.copy(dw[:], ps[:, SB0 + 1, P:P + TAPS * CC]).then_inc(vec_made, 1)
                if n == S_GLU:
                    act.wait_ge(vec_made, 1)
                    for c in range(CC):
                        act.wait_ge(glu_tr, c + 1)
                        nc.scalar.activation(conv[:, c], ps[:, TB + c, T:2 * T], ACT.Sigmoid,
                                             bias=vec[:, V_BGLU + CC + c:V_BGLU + CC + c + 1]).then_inc(glu_sig, 1)
                if n == S_QT:
                    qk_out(0, TB)
                if n == S_KT:
                    qk_out(1, SB0)
                if n < U_ATTN and n % 2 == 1 and n // 2 < GA:
                    take(n // 2)
                if S_ATT + 1 <= n <= S_ATT + PAIRS:
                    probs_out(n - S_ATT - 1)
                if S_ATT <= n < S_ATT + PAIRS:
                    exps(n - S_ATT)
                if n == S_ATT + PAIRS - 1:
                    take(GA)
                if n < U_ATTN and n % 2 == 1 and n // 2 > GA:
                    take(n // 2)
                if n == S_OT:
                    act.wait_ge(o_tr, 1)
                    nc.scalar.copy(b_hi[:, 0:CC], chunks(TB)).then_inc(o_hi, 1)
                if n == S_LN + 1:
                    for c in range(CC):
                        act.wait_ge(zn_tr, 1)
                        nc.scalar.activation(conv[:, c], chunks(SB0)[:, c], ACT.Sigmoid, bias=vec[:, V_LNB + c:V_LNB + c + 1],
                                             scale=vec[:, V_LNG + c:V_LNG + c + 1]).then_inc(silu_sig, 1)
                    act.wait_ge(silu_made, CC + 1)
                    nc.scalar.copy(b_hi[:, CC:2 * CC], silu_x).then_inc(cz_hi, 1)
                if n in (U_CONV + 1, U_OUT):
                    col, bank = n - U_CONV - 1, (TB, SB0)[n - U_CONV - 1]
                    for t in range(TT):
                        act.wait_ge(m_tr, 2 * col + t + 1)
                        nc.scalar.copy(a_hi[:, 4 * col:4 * col + 4, t * P:t * P + P], tile_chunks(bank, t)).then_inc(m_hi, 1)
                if n in (U_OUT + 3, U_FF):
                    half = 0 if n == U_OUT + 3 else 1
                    act.wait_ge(h_tr, half + 1)
                    for c in range(4):
                        k = 4 * half + c
                        nc.scalar.activation(b_hi[:, k], chunks(TB)[:, c], ACT.Copy,
                                             scale=vec[:, V_GFFN + k:V_GFFN + k + 1]).then_inc(h_hi, 1)
                if n == U_FF:
                    for t in range(TT):
                        nc.scalar.activation(nat[:, t], res[:, t], ACT.Square,
                                             accum_out=sq_sum[:, 1, t:t + 1]).then_inc(sq_made, 1)

            def relu_out():
                for t in range(TT):
                    last = nc.scalar.activation(nat[:, t, 0:W], ps[:, SB0 + t], ACT.Relu, scale=rstd[:, 2, t:t + 1])
                last.then_inc(relu_made, 1)

            def hidden_high(blocks):
                for t in range(TT):
                    act.wait_ge(f_tr, blocks * 2 + (t - 1))
                    nc.scalar.copy(a_hi[:, 0:4, t * P:t * P + P], tile_chunks(TB, t)).then_inc(f_hi, 1)

            act.wait_ge(used, U_LOOP)
            act.wait_ge(rstd_made, 3)
            relu_out()
            with act.Fori(0, FB - 1) as i:
                for j in range(4):
                    slot = (j + AHEAD) % SLOTS
                    act.wait_ge(raw_full[slot], i * 16 + 16 * ((U_LOOP + j + AHEAD) // SLOTS + 1))
                    act.wait_ge(used, i * 4 + (U_LOOP + j + AHEAD - SLOTS + 1))
                    nc.scalar.copy(w_hi[:, slot], raw[:, slot]).then_inc(hi_made, 1)
                    if j == 0:
                        hidden_high(i + 1)
                    if j == 1:
                        act.wait_ge(used, i * 4 + (U_LOOP + 2))
                        act.wait_ge(sq_hidden, i + 1)
                        relu_out()
            hidden_high(FB)
            for t in range(TT):
                for col in range(2):
                    act.wait_ge(y_made, 2 * t + col + 1)
                    nc.scalar.activation(nat[:, t, col * W:col * W + W], res[:, t, col * W:col * W + W], ACT.Square,
                                         accum_out=sq_sum[:, 2, 2 * t + col:2 * t + col + 1]).then_inc(sq_made, 1)
                act.wait_ge(rstd_made, 4 + t)
                act.wait_ge(y_scaled, 2 * t + 2)
                nc.scalar.activation(res[:, t, W:D], gates[:, 0, t, W:D], ACT.Copy,
                                     scale=rstd[:, 3 + t, 0:1]).then_inc(out_made_act, 1)
                act.wait_ge(out_made_act, t + 1)
                act.dma_start(out_v[:, t, W:D], res[:, t, W:D]).then_inc(stored, 16)

        @block.vector
        def _(dve):
            def low(n):
                if n in POOL_LO:
                    return
                dve.wait_ge(hi_made, n + 1)
                nc.vector.tensor_tensor(w_lo[:, n % SLOTS], raw[:, n % SLOTS], w_hi[:, n % SLOTS].bitcast(F32),
                                        ALU.subtract).then_inc(lo_made, 1)

            nc.vector.memset(zero_b[:], 0.0).then_inc(zero_made, 1)
            dve.wait_ge(first_full, 16)
            nc.vector.tensor_copy(w_hi[:, 0, 0:2], raw[:, 0, 0:2]).then_inc(first_hi, 1)
            dve.wait_ge(gmix_made, 1)
            for pair in range(4):
                dve.wait_ge(xt_hi, 2 * pair + 2)
                for k in (2 * pair, 2 * pair + 1):
                    nc.vector.scalar_tensor_tensor(out=a_lo[:, k], in0=x_chunk(k), scalar=gmix[:, k:k + 1],
                                                   in1=a_hi[:, k].bitcast(F32), op0=ALU.mult,
                                                   op1=ALU.subtract).then_inc(xt_lo, 1)
                if pair == 0:
                    dve.wait_ge(first_hi, 1)
                    nc.vector.tensor_tensor(w_lo[:, 0, 0:2], raw[:, 0, 0:2], w_hi[:, 0, 0:2].bitcast(F32),
                                            ALU.subtract).then_inc(first_lo, 1)
                if pair == 1:
                    dve.wait_ge(hi_made, 1)
                    nc.vector.tensor_tensor(w_lo[:, 0, 2:HK], raw[:, 0, 2:HK], w_hi[:, 0, 2:HK].bitcast(F32),
                                            ALU.subtract).then_inc(lo_made, 1)
            low(1)
            dve.wait_ge(sq_made, TT)
            nc.vector.tensor_scalar(ms[:, 0], sq_sum[:, 0, 0:TT], 1.0 / D, EPS, ALU.mult, ALU.add).then_inc(ms_made, 1)

            def conv_products(step):
                for m in conv_share(step):
                    tap, c = divmod(m, CC)
                    if tap == 0:
                        nc.vector.tensor_scalar(conv[:, c], z[:, c, 0:T], dw[:, c:c + 1], vec[:, V_BDW + c:V_BDW + c + 1],
                                                ALU.mult, ALU.add).then_inc(conv_step, 1)
                    else:
                        dve.wait_ge(conv_step, m - CC + 1)
                        nc.vector.scalar_tensor_tensor(out=conv[:, c], in0=z[:, c, tap:tap + T], scalar=dw[:, m:m + 1],
                                                       in1=conv[:, c], op0=ALU.mult, op1=ALU.add).then_inc(conv_step, 1)

            def row_max(p):
                dve.wait_ge(scored, p + 1)
                nc.vector.tensor_reduce(smax[:, p, 0:2], ps[:, SB0:SB0 + 2, 0:256], AX.X,
                                        ALU.max).then_inc(max_made, 1)
                nc.vector.tensor_reduce(smax[:, p, 2:4], ps[:, SB0:SB0 + 2, 256:384], AX.X,
                                        ALU.max).then_inc(max_made, 1)
                dve.wait_ge(max_made, 2 * p + 2)
                nc.vector.tensor_scalar(nbias[:, p], smax[:, p], -SCALE, None, ALU.mult).then_inc(bias_made, 1)

            def inverse(p):
                dve.wait_ge(exp_made, p + 1)
                nc.vector.reciprocal(rinv[:, p], psums[:, p]).then_inc(rinv_made, 1)

            def o_out(p):
                dve.wait_ge(pv_done, p + 1)
                dve.wait_ge(rinv_made, p + 1)
                for s in range(2):
                    last = nc.vector.tensor_tensor(
                        o_nat[:, 1 - s, 128 * p:128 * p + 128].rearrange("p (h d) -> p h d", h=2),
                        ps[:, SB0:SB0 + 2, 384 + HD * s:384 + HD * s + HD],
                        rinv[:, p, 2 * s:2 * s + 2].rearrange("p (h a) -> p h a", a=1).to_broadcast([P, 2, HD]), ALU.mult)
                last.then_inc(o_made, 1)

            def tile_products(n, t):
                if t == 0:
                    dve.wait_ge(tile_done, n - U_CONV + 1)
                else:
                    dve.wait_ge(used, n + 1)

            for n in range(U_LOOP):
                if n < S_ATT or n == S_LN + 1:
                    low(n + AHEAD)
                if n == S_GLU:
                    for c in range(CC):
                        dve.wait_ge(glu_sig, c + 1)
                        nc.vector.scalar_tensor_tensor(out=z[:, c, PAD:PAD + T], in0=ps[:, TB + c, 0:T],
                                                       scalar=vec[:, V_BGLU + c:V_BGLU + c + 1], in1=conv[:, c],
                                                       op0=ALU.add, op1=ALU.mult).then_inc(z_made, 1)
                    dve.wait_ge(z_made, CC)
                    dve.wait_ge(vec_made, 2)
                    dve.wait_ge(const_made, 4)
                if S_ATT + 2 <= n < S_ATT + 2 + PAIRS:
                    o_out(n - S_ATT - 2)
                if S_ATT + 1 <= n < S_ATT + 1 + PAIRS:
                    inverse(n - S_ATT - 1)
                if S_ATT <= n < S_ATT + PAIRS:
                    row_max(n - S_ATT)
                if n == S_OT:
                    dve.wait_ge(o_hi, 1)
                    nc.vector.tensor_tensor(b_lo[:, 0:CC], chunks(TB), b_hi[:, 0:CC].bitcast(F32),
                                            ALU.subtract).then_inc(o_lo, 1)
                if n == S_LN:
                    dve.wait_ge(conv_tr, 1)
                    for t in range(TT):
                        nc.vector.bn_stats(stats[:, t], ps[:, TB + t]).then_inc(ln_chain, 1)
                    dve.wait_ge(ln_chain, TT)
                    for t in range(TT):
                        last = nc.vector.bn_aggr(mean_var[:, t], stats[:, t])
                    last.then_inc(zn_made, 1)
                    dve.wait_ge(zn_made, 1)
                    nc.vector.tensor_scalar(ln_var[:], mean_var[:, :, 1], EPS, None, ALU.add).then_inc(ms_made, 1)
                    low(n + AHEAD)
                    dve.wait_ge(rstd_made, 2)
                    for t in range(TT):
                        nc.vector.tensor_scalar(zn[:, t], ps[:, TB + t], mean_var[:, t, 0:1], rstd[:, 1, t:t + 1],
                                                ALU.subtract, ALU.mult).then_inc(zn_made, 1)
                if n == S_LN + 1:
                    dve.wait_ge(zn_tr, 1)
                    for c in range(CC):
                        dve.wait_ge(silu_sig, c // 2 * 2 + 2)
                        nc.vector.tensor_scalar(silu_x[:, c], chunks(SB0)[:, c], vec[:, V_LNG + c:V_LNG + c + 1],
                                                vec[:, V_LNB + c:V_LNB + c + 1], ALU.mult, ALU.add).then_inc(silu_made, 1)
                    dve.wait_ge(silu_made, CC)
                    nc.vector.tensor_tensor(silu_x, silu_x, conv[:], ALU.mult).then_inc(silu_made, 1)
                    dve.wait_ge(cz_hi, 1)
                    nc.vector.tensor_tensor(b_lo[:, CC:2 * CC], silu_x, b_hi[:, CC:2 * CC].bitcast(F32),
                                            ALU.subtract).then_inc(cz_lo, 1)
                if n in (U_ATTN, U_ATTN + 1):
                    col = n - U_ATTN
                    dve.wait_ge(used, n + 1)
                    dve.wait_ge(evac, len(ORDER))
                    for t in range(TT):
                        last = nc.vector.tensor_tensor(nat[:, t, col * W:col * W + W], ps[:, 2 * (1 - col) + t],
                                                       gates[:, 0, t, col * W:col * W + W], ALU.mult)
                    last.then_inc(m_attn, 1)
                if n in (U_CONV + 1, U_OUT):
                    col, bank = n - U_CONV - 1, (TB, SB0)[n - U_CONV - 1]
                    for t in range(TT):
                        dve.wait_ge(m_hi, 2 * col + t + 1)
                        tok = slice(t * P, t * P + P)
                        nc.vector.tensor_tensor(a_lo[:, 4 * col:4 * col + 4, tok], tile_chunks(bank, t),
                                                a_hi[:, 4 * col:4 * col + 4, tok].bitcast(F32),
                                                ALU.subtract).then_inc(m_lo, 1)
                if n in (U_CONV, U_CONV + 1):
                    col = n - U_CONV
                    dve.wait_ge(m_bias, col + 1)
                    for t in range(TT):
                        tile_products(n, t)
                        g = gates[:, 1, t, col * W:col * W + W]
                        nc.vector.tensor_tensor(g, ps[:, 2 * (1 - col) + t], g, ALU.mult).then_inc(m_conv, 1)
                        dve.wait_ge(m_conv, 2 * col + t + 1)
                        part = nat[:, t, col * W:col * W + W]
                        nc.vector.tensor_tensor(part, part, gates[:, 1, t, col * W:col * W + W], ALU.add).then_inc(merged, 1)
                if n in (U_OUT + 3, U_FF):
                    half = 0 if n == U_OUT + 3 else 1
                    for c in range(4):
                        k = 4 * half + c
                        dve.wait_ge(h_hi, k // 2 * 2 + 2)
                        nc.vector.scalar_tensor_tensor(out=b_lo[:, k], in0=chunks(TB)[:, c],
                                                       scalar=vec[:, V_GFFN + k:V_GFFN + k + 1],
                                                       in1=b_hi[:, k].bitcast(F32), op0=ALU.mult,
                                                       op1=ALU.subtract).then_inc(h_lo, 1)
                if n in (U_OUT + 2, U_OUT + 3):
                    col = n - U_OUT - 2
                    for t in range(TT):
                        tile_products(n, t)
                        part = res[:, t, col * W:col * W + W]
                        nc.vector.tensor_tensor(part, ps[:, 2 * (1 - col) + t], part, ALU.add).then_inc(res2, 1)
                if n == U_FF:
                    dve.wait_ge(sq_made, 2 * TT)
                    nc.vector.tensor_scalar(ms[:, 1], sq_sum[:, 1, 0:TT], 1.0 / D, EPS, ALU.mult, ALU.add).then_inc(ms_made, 1)
                if n >= S_ATT and n not in (S_LN, S_LN + 1):
                    low(n + AHEAD)
                conv_products(n)

            def hidden_low(blocks):
                for t in range(TT):
                    tok = slice(t * P, t * P + P)
                    dve.wait_ge(f_hi, blocks * 2 + (t - 1))
                    nc.vector.tensor_tensor(a_lo[:, 0:4, tok], tile_chunks(TB, t), a_hi[:, 0:4, tok].bitcast(F32),
                                            ALU.subtract).then_inc(f_lo, 1)

            with dve.Fori(0, FB - 1) as i:
                for j in range(4):
                    slot = (j + AHEAD) % SLOTS
                    dve.wait_ge(hi_made, i * 4 + (U_LOOP + j + AHEAD + 1))
                    nc.vector.tensor_tensor(w_lo[:, slot], raw[:, slot], w_hi[:, slot].bitcast(F32),
                                            ALU.subtract).then_inc(lo_made, 1)
                    if j == 0:
                        hidden_low(i + 1)
            hidden_low(FB)
            dve.wait_ge(bc_full, 32)
            for t in range(TT):
                for col in range(2):
                    part = slice(col * W, col * W + W)
                    dve.wait_ge(ff_done, 2 * t + col + 1)
                    nc.vector.tensor_tensor(res[:, t, part], ps[:, 2 * t + col], res[:, t, part], ALU.add).then_inc(y_made, 1)
                    dve.wait_ge(y_made, 2 * t + col + 1)
                    nc.vector.tensor_tensor(gates[:, 0, t, part], res[:, t, part], gfin_bc[:, part],
                                            ALU.mult).then_inc(y_scaled, 1)
                    dve.wait_ge(sq_made, 2 * TT + 2 * t + col + 1)
                    if col == 0:
                        nc.vector.tensor_scalar(sq_sum[:, 1, 2 + t:3 + t], sq_sum[:, 2, 2 * t:2 * t + 1], 1.0 / D, EPS,
                                                ALU.mult, ALU.add).then_inc(mean_part, 1)
                dve.wait_ge(mean_part, t + 1)
                nc.vector.scalar_tensor_tensor(out=ms[:, 2, t:t + 1], in0=sq_sum[:, 2, 2 * t + 1:2 * t + 2], scalar=1.0 / D,
                                               in1=sq_sum[:, 1, 2 + t:3 + t], op0=ALU.mult, op1=ALU.add).then_inc(ms_made, 1)
                dve.wait_ge(rstd_made, 4 + t)
                nc.vector.tensor_scalar(res[:, t, 0:W], gates[:, 0, t, 0:W], rstd[:, 3 + t, 0:1], None,
                                        ALU.mult).then_inc(out_made, 1)

        @block.tensor
        def _(pe):
            def transpose(dst, src):
                return nc.tensor.transpose(dst, src, ident[0:src.shape[0], 0:src.shape[0]])

            def transpose_chunks(bank, source):
                for c in range(4):
                    for t in range(TT):
                        last = transpose(chunks(bank)[:, c, t * P:t * P + P], source(t, c))
                return last

            def products(slot, k, hi, lo, bank, t, start, stop, low_sem=None):
                dst = ps[:, bank]
                tok = slice(t * P, t * P + P)
                nc.tensor.matmul(dst, lo[:, tok], w_hi[:, slot, k], start=start, stop=False)
                nc.tensor.matmul(dst, hi[:, tok], w_hi[:, slot, k], start=False, stop=False)
                if low_sem is not None:
                    pe.wait_ge(low_sem, 1)
                return nc.tensor.matmul(dst, hi[:, tok], w_lo[:, slot, k], start=False, stop=stop)

            def weights(n):
                dve, pool = low_count(n)
                pe.wait_ge(hi_made, n + 1)
                pe.wait_ge(lo_made, dve)
                if pool:
                    pe.wait_ge(lo_made_pool, pool)

            def unit(n, hi, lo, first, bank, start, stop, between=None, place=HK - 1, tiles=False):
                weights(n)
                for t in range(TT):
                    for k in range(HK):
                        last = products(n % SLOTS, k, hi[:, first + k], lo[:, first + k], bank(t), t,
                                        start and k == 0, stop and k == HK - 1)
                        if tiles and t == 0 and k == HK - 1:
                            last.then_inc(tile_done, 1)
                        if t == 0 and k == place and between is not None:
                            between()
                last.then_inc(used, 1)

            pe.wait_ge(zero_made, 1)
            for _ in range(WARM):
                nc.tensor.matmul(ps[:, 0], zero_b[:, 0:P], zero_b[:], start=True, stop=True)
            pe.wait_ge(ident_made, 1)
            pe.wait_ge(gmix_full, 16)
            transpose(ps[:, SB0, 0:KD], gmix_rows[:]).then_inc(gmix_tr, 1)
            for t in range(TT):
                pe.wait_ge(x_full[t], 16)
                for k in range(KD):
                    last = transpose(x_chunk(k)[:, t * P:t * P + P], res[:, t, k * P:k * P + P])
                    if t == TT - 1 and k % 2 == 1:
                        last.then_inc(x_tr, 1)

            for k in range(HK):
                if k == 0:
                    pe.wait_ge(first_hi, 1)
                    pe.wait_ge(xt_lo, 2)
                if k == 2:
                    pe.wait_ge(xt_lo, 4)
                    weights(0)
                for t in range(TT):
                    last = products(0, k, a_hi[:, k], a_lo[:, k], t, t, k == 0, False,
                                    first_lo if k == 0 and t == 0 else None)
            last.then_inc(used, 1)

            def scores(p):
                if p >= 2:
                    pe.wait_ge(o_made, p - 1)
                for s, at, keys in ((1, 0, 256), (0, 256, 128)):
                    for h in range(2):
                        rows = slice(HD * h, HD * h + HD)
                        nc.tensor.matmul(ps[:, SB0 + h, at:at + keys], qk_t[rows, 0, p, s * P:s * P + P],
                                         qk_t[rows, 1, p, 0:keys], start=True, stop=False)
                    for h in range(2):
                        last = nc.tensor.matmul(ps[:, SB0 + h, at:at + keys], ident_b[:], mask_b[:, T - keys:T],
                                                start=False, stop=True)
                last.then_inc(scored, 1)

            def probs_transposed(p):
                pe.wait_ge(exp_made, p + 1)
                if p:
                    pe.wait_ge(pt_made, p)
                for blk in range(6):
                    o = blk * P
                    last = transpose(ps[:, TB + o // W, o % W:o % W + P], probs[:, o:o + P])
                last.then_inc(p_tr, 1)

            def values(p):
                pe.wait_ge(pt_made, p + 1)
                if p:
                    pe.wait_ge(o_made, p)
                if p + 2 <= PAIRS:
                    pe.wait_ge(exp_made, p + 2)
                for s in range(2):
                    for h in range(2):
                        head = slice(HD * (2 * p + h), HD * (2 * p + h) + HD)
                        o = 384 + HD * s
                        n_keys = 2 - s
                        for kb in range(n_keys):
                            at = 256 * h + P * kb if s == 0 else 512 + P * h
                            last = nc.tensor.matmul(ps[:, SB0 + h, o:o + HD], probs_t[:, at:at + P], v_nat[:, kb, head],
                                                    start=kb == 0, stop=kb == n_keys - 1)
                last.then_inc(pv_done, 1)

            for n in range(1, U_ATTN):
                b, half = divmod(n, 2)
                if n == 1:
                    pe.wait_ge(xt_lo, KD)
                if half == 0 and b >= 2:
                    pe.wait_ge(evac, b - 1)
                unit(n, a_hi, a_lo, HK * half, lambda t: 2 * (b % 2) + t, half == 0, half == 1)
                if n == S_VEC:
                    pe.wait_ge(vec_full, 16 * 6)
                    transpose(ps[:, SB0 + 1, 0:VROWS], vec_rows[:])
                    transpose(ps[:, SB0 + 1, P:P + TAPS * CC], dw_rows[:]).then_inc(vec_tr, 1)
                if n == S_GLU:
                    pe.wait_ge(vec_made, 2)
                    pe.wait_ge(evac, UG + 1)
                    for c in range(CC):
                        for part in range(2):
                            for t in range(TT):
                                last = transpose(ps[:, TB + c, part * T + t * P:part * T + t * P + P],
                                                 nat[:, t, part * W + c * P:part * W + c * P + P])
                        last.then_inc(glu_tr, 1)
                if n == S_QT:
                    pe.wait_ge(evac, Q + 1)
                    pe.wait_ge(z_made, CC)
                    transpose_chunks(TB, lambda t, c: nat[:, t, c * P:c * P + P]).then_inc(qk_tr, 1)
                if n == S_KT:
                    pe.wait_ge(evac, K + 1)
                    transpose_chunks(SB0, lambda t, c: nat[:, t, W + c * P:W + c * P + P]).then_inc(qk_tr, 1)
                if S_ATT + 2 <= n < S_ATT + 2 + PAIRS:
                    if n == S_ATT + 2:
                        pe.wait_ge(evac, V + 1)
                    values(n - S_ATT - 2)
                if S_ATT + 1 <= n <= S_ATT + PAIRS:
                    probs_transposed(n - S_ATT - 1)
                if S_ATT <= n < S_ATT + PAIRS:
                    if n == S_ATT:
                        pe.wait_ge(qk_made, 2)
                        pe.wait_ge(ident_made, 3)
                    scores(n - S_ATT)
                if n == S_OT:
                    pe.wait_ge(o_made, PAIRS)
                    transpose_chunks(TB, lambda t, c: o_nat[:, t, c * P:c * P + P]).then_inc(o_tr, 1)
                if n == S_LN:
                    pe.wait_ge(conv_step, TAPS * CC)
                    pe.wait_ge(o_lo, 1)
                    for t in range(TT):
                        for c in range(CC):
                            last = transpose(ps[:, TB + t, c * P:c * P + P], conv[:, c, t * P:t * P + P])
                    last.then_inc(conv_tr, 1)
                if n == S_LN + 1:
                    pe.wait_ge(zn_made, 1 + TT)
                    transpose_chunks(SB0, lambda t, c: zn[:, t, c * P:c * P + P]).then_inc(zn_tr, 1)

            def merged_transposed(col, bank):
                for t in range(TT):
                    pe.wait_ge(merged, 2 * col + t + 1)
                    for c in range(4):
                        last = transpose(tile_chunks(bank, t)[:, c], nat[:, t, col * W + c * P:col * W + c * P + P])
                    last.then_inc(m_tr, 1)

            def res_transposed(col):
                pe.wait_ge(res2, 2 * col + 2)
                transpose_chunks(TB, lambda t, c: res[:, t, col * W + c * P:col * W + c * P + P]).then_inc(h_tr, 1)

            for col in range(2):
                pe.wait_ge(o_lo, 1)
                pe.wait_ge(evac, len(ORDER) - 1 + col)
                unit(U_ATTN + col, b_hi, b_lo, 0, lambda t: 2 * (1 - col) + t, True, True)
            for col in range(2):
                pe.wait_ge(cz_lo, 1)
                pe.wait_ge(m_attn, col + 1)
                unit(U_CONV + col, b_hi, b_lo, CC, lambda t: 2 * (1 - col) + t, True, True,
                     (lambda: merged_transposed(0, TB)) if col == 1 else None, tiles=True)
            for half in range(2):
                for col in range(2):
                    if half == 0:
                        pe.wait_ge(m_lo, 2)
                        pe.wait_ge(merged, 2 * col + 2)
                    else:
                        pe.wait_ge(m_lo, 4)
                    unit(U_OUT + 2 * half + col, a_hi, a_lo, HK * half, lambda t: 2 * (1 - col) + t, half == 0, half == 1,
                         ((lambda: merged_transposed(1, SB0)) if half == 0 and col == 0 else
                          (lambda: res_transposed(0)) if half == 1 and col == 1 else None),
                         place=1 if half == 1 else HK - 1, tiles=True)
            for half in range(2):
                pe.wait_ge(h_lo, 4 * half + 4)
                unit(U_FF + half, b_hi, b_lo, HK * half, lambda t: SB0 + t, half == 0, half == 1,
                     (lambda: res_transposed(1)) if half == 0 else None, place=1)

            def hidden_transposed():
                for t in range(TT):
                    for c in range(4):
                        last = transpose(tile_chunks(TB, t)[:, c], nat[:, t, W + c * P:W + c * P + P])
                    last.then_inc(f_tr, 1)

            for bank in range(4):
                nc.tensor.matmul(ps[:, bank], zero_b[:, 0:P], zero_b[:], start=True, stop=False)

            pools = len(POOL_LO)
            with pe.Fori(0, FB - 1) as i:
                for j in range(4):
                    pe.wait_ge(hi_made, i * 4 + (U_LOOP + j + 1))
                    pe.wait_ge(lo_made, i * 4 + (U_LOOP + j + 1 - pools))
                    if j == 0:
                        pe.wait_ge(relu_made, i + 1)
                    if j == 2:
                        pe.wait_ge(f_lo, i * 2 + 2)
                    for t in range(TT):
                        for k in range(HK):
                            if j < 2:
                                last = products(j, k, b_hi[:, HK * j + k], b_lo[:, HK * j + k], SB0 + t, t,
                                                j == 0 and k == 0, j == 1 and k == HK - 1)
                            else:
                                last = products(j, k, a_hi[:, k], a_lo[:, k], 2 * t + j - 2, t, False, False)
                    last.then_inc(used, 1)
                    if j == 0:
                        pe.wait_ge(sq_hidden, i + 1)
                        hidden_transposed()
            pe.wait_ge(sq_hidden, FB)
            hidden_transposed()
            weights(U_LAST + 1)
            for t in range(TT):
                pe.wait_ge(f_lo, 2 * (FB - 1) + t + 1)
                for col in range(2):
                    for k in range(HK):
                        last = products(col, k, a_hi[:, k], a_lo[:, k], 2 * t + col, t, False, k == HK - 1)
                    last.then_inc(ff_done, 1)


_INS = ['x', 'g_mix', 'w_in', 'b_glu', 'w_dw', 'b_dw', 'ln_g', 'ln_b', 'w_conv_pw', 'b_conv_pw',
        'w_attn_up', 'w_out', 'g_ffn', 'w_ff1', 'w_ff2', 'g_final']
_OUTS = [((1, 256, 1024), 'float32')]


def kernel(**inputs):
    import numpy as _np
    import concourse.bacc as _bacc
    from concourse import mybir as _mybir
    from concourse.bass_utils import run_bass_kernel_spmd as _run

    nc = _bacc.Bacc("TRN2", target_bir_lowering=False, num_devices=1)
    arrays, args = {}, []
    for name in _INS:
        a = _np.ascontiguousarray(inputs[name])
        arrays[f"in_{name}_dram"] = a
        args.append(nc.dram_tensor(f"in_{name}_dram", a.shape, _mybir.dt.from_np(a.dtype), kind="ExternalInput").ap())
    for i, (shape, dtype) in enumerate(_OUTS):
        dt = _mybir.dt.from_np(_np.dtype(dtype))
        args.append(nc.dram_tensor(f"out_{i}_dram", shape, dt, kind="ExternalOutput").ap())
    build(nc, *args)
    r = _run(nc, [arrays], core_ids=[0])
    got = tuple(r.results[0][f"out_{i}_dram"] for i in range(len(_OUTS)))
    return got[0]
```
